# Optimizing a Trainium2 kernel written in Bass

```python
import jax, jax.numpy as jnp
from jax import lax
import numpy as np

D_MODEL = 2048
BATCH = 1
SEQ = 256
DEPTH = 1
DEC_BATCH = 8
DEC_SEQ = 1
PAST_LEN = 2048
PAGE_SIZE = 128

N_META = 16
N_HEADS = 8
DK = D_MODEL // 16
DV = D_MODEL // N_HEADS
D_CONV = D_MODEL
CONV_W = 3
D_FF = 11 * D_MODEL // 4
CHUNK = 128
EPS = 1e-6
D_IN_PROJ = 4 * D_CONV + 2 * N_HEADS * DK + 3 * N_HEADS * DV + 2 * N_HEADS

kernel_name = 'hybrid_shortconv_mlstm_decoder_step'

def rmsnorm(x, g):
    xf = x.astype(jnp.float32)
    y = xf * lax.rsqrt(jnp.mean(xf * xf, axis=-1, keepdims=True) + EPS)
    return (y * g.astype(jnp.float32)).astype(x.dtype)

def causal_dwconv(u, buf, w):
    t = u.shape[1]
    full = jnp.concatenate([buf.astype(u.dtype), u], axis=1)
    y = full[:, 0:t] * w[0]
    for j in range(1, CONV_W):
        y = y + full[:, j:j + t] * w[j]
    return y, full[:, t:]

def mlstm_chunk(state, inp):
    c_prev, n_prev, m_prev = state
    q, k, v, ig, lf = inp
    l = q.shape[2]
    b = jnp.cumsum(lf, axis=-1)
    causal = jnp.tril(jnp.ones((l, l), dtype=bool))
    dmat = jnp.where(causal, b[..., :, None] - b[..., None, :] + ig[..., None, :], -jnp.inf)
    m_t = jnp.maximum(b + m_prev[..., None], jnp.max(dmat, axis=-1))
    w_ts = jnp.exp(dmat - m_t[..., None])
    s = jnp.einsum('bhtd,bhsd->bhts', q, k) * w_ts
    decay = jnp.exp(b + m_prev[..., None] - m_t)
    num = decay[..., None] * jnp.einsum('bhtd,bhdv->bhtv', q, c_prev) + jnp.einsum('bhts,bhsv->bhtv', s, v)
    den = decay * jnp.einsum('bhtd,bhd->bht', q, n_prev) + jnp.sum(s, axis=-1)
    h = num / jnp.maximum(jnp.abs(den), jnp.exp(-m_t))[..., None]
    m_last = m_t[..., -1]
    g = jnp.exp(b[..., -1:] - b + ig - m_last[..., None])
    carry = jnp.exp(b[..., -1] + m_prev - m_last)
    c_new = carry[..., None, None] * c_prev + jnp.einsum('bhs,bhsd,bhsv->bhdv', g, k, v)
    n_new = carry[..., None] * n_prev + jnp.einsum('bhs,bhsd->bhd', g, k)
    return (c_new, n_new, m_last), h

def mlstm_sequence(q, k, v, ig, lf, state, first):
    state, h_first = mlstm_chunk(state, (q[:, :, :first], k[:, :, :first], v[:, :, :first],
                                         ig[:, :, :first], lf[:, :, :first]))
    rest = q.shape[2] - first
    if rest == 0:
        return h_first, state
    nc = rest // CHUNK

    def to_chunks(a):
        a = a[:, :, first:]
        a = a.reshape(a.shape[0], a.shape[1], nc, CHUNK, *a.shape[3:])
        return jnp.moveaxis(a, 2, 0)

    state, h_rest = lax.scan(mlstm_chunk, state, tuple(to_chunks(a) for a in (q, k, v, ig, lf)))
    h_rest = jnp.moveaxis(h_rest, 0, 2)
    h_rest = h_rest.reshape(h_rest.shape[0], h_rest.shape[1], rest, DV)
    return jnp.concatenate([h_first, h_rest], axis=2), state

def block(x, c0, n0, m0, sc0, fc0, first, norm1_g, w_in, b_if, w_shortconv, w_out,
          norm2_g, w_up, w_ffconv, w_down):
    bsz, t, _ = x.shape
    h = rmsnorm(x, norm1_g)
    z = h @ w_in
    sizes = (D_CONV, D_CONV, D_CONV, N_HEADS * DK, N_HEADS * DK, N_HEADS * DV,
             N_HEADS * DV, 2 * N_HEADS, D_CONV, N_HEADS * DV)
    u, cg, bg, q, k, v, o, gif, g_a, g_b = jnp.split(z, np.cumsum(sizes)[:-1].tolist(), axis=-1)
    conv_out, sc = causal_dwconv(cg * u, sc0, w_shortconv)
    a_out = bg * conv_out
    def to_heads(a, d):
        return a.reshape(bsz, t, N_HEADS, d).transpose(0, 2, 1, 3).astype(jnp.float32)
    qh = to_heads(q, DK)
    kh = to_heads(k, DK) * (DK ** -0.5)
    vh = to_heads(v, DV)
    gif = (gif + b_if).astype(jnp.float32).transpose(0, 2, 1)
    ig = gif[:, :N_HEADS]
    lf = jax.nn.log_sigmoid(gif[:, N_HEADS:])
    state0 = (c0.astype(jnp.float32), n0.astype(jnp.float32), m0.astype(jnp.float32))
    hb, (c, n, m) = mlstm_sequence(qh, kh, vh, ig, lf, state0, first)
    hb = hb.transpose(0, 2, 1, 3).reshape(bsz, t, N_HEADS * DV).astype(x.dtype)
    b_out = jax.nn.sigmoid(o) * hb
    mix = jax.nn.sigmoid(g_a) * a_out + jax.nn.sigmoid(g_b) * b_out
    x = x + mix @ w_out
    h2 = rmsnorm(x, norm2_g)
    up, fc = causal_dwconv(h2 @ w_up, fc0, w_ffconv)
    x = x + (jax.nn.silu(up[..., D_FF:]) * up[..., :D_FF]) @ w_down
    return x, c, n, m, sc, fc

def setup_inputs(seed: int = 0) -> dict:
    key = jax.random.key(seed)
    ks = jax.random.split(key, 20)

    def nrm(k, shape, scale):
        return jax.random.normal(k, shape, jnp.float32) * scale

    return {
        'x_prompt': nrm(ks[0], (BATCH, SEQ, D_MODEL), 1.0),
        'x_sample': nrm(ks[1], (DEC_BATCH, DEC_SEQ, D_MODEL), 1.0),
        'state_mlstm_C': nrm(ks[2], (DEPTH, DEC_BATCH, N_HEADS, DK, DV), DK ** -0.5),
        'state_mlstm_n': nrm(ks[3], (DEPTH, DEC_BATCH, N_HEADS, DK), DK ** -0.5),
        'state_mlstm_m': nrm(ks[4], (DEPTH, DEC_BATCH, N_HEADS), 1.0),
        'state_shortconv': nrm(ks[5], (DEPTH, DEC_BATCH, CONV_W - 1, D_CONV), 0.5),
        'state_ffnconv': nrm(ks[6], (DEPTH, DEC_BATCH, CONV_W - 1, 2 * D_FF), 0.5),
        'meta_tokens': nrm(ks[7], (N_META, D_MODEL), 1.0),
        'norm1_g': 1.0 + nrm(ks[8], (DEPTH, D_MODEL), 0.02),
        'w_in': nrm(ks[9], (DEPTH, D_MODEL, D_IN_PROJ), D_MODEL ** -0.5),
        'b_if': jnp.concatenate([nrm(ks[10], (DEPTH, N_HEADS), 0.1),
                                 3.0 + nrm(ks[11], (DEPTH, N_HEADS), 0.5)], axis=-1),
        'w_shortconv': nrm(ks[12], (DEPTH, CONV_W, D_CONV), CONV_W ** -0.5),
        'w_out': nrm(ks[13], (DEPTH, D_MODEL, D_MODEL), D_MODEL ** -0.5),
        'norm2_g': 1.0 + nrm(ks[14], (DEPTH, D_MODEL), 0.02),
        'w_up': nrm(ks[15], (DEPTH, D_MODEL, 2 * D_FF), D_MODEL ** -0.5),
        'w_ffconv': nrm(ks[16], (DEPTH, CONV_W, 2 * D_FF), CONV_W ** -0.5),
        'w_down': nrm(ks[17], (DEPTH, D_FF, D_MODEL), D_FF ** -0.5),
        'norm_f_g': 1.0 + nrm(ks[18], (D_MODEL,), 0.02),
    }

def reference(x_prompt, x_sample, state_mlstm_C, state_mlstm_n, state_mlstm_m, state_shortconv,
              state_ffnconv, meta_tokens, norm1_g, w_in, b_if, w_shortconv, w_out, norm2_g,
              w_up, w_ffconv, w_down, norm_f_g):
    bsz = x_prompt.shape[0]
    meta = jnp.broadcast_to(meta_tokens.astype(x_prompt.dtype)[None], (bsz, N_META, D_MODEL))
    xp = jnp.concatenate([meta, x_prompt], axis=1)
    xs = x_sample
    pc, pn, pm, psc, pfc = [], [], [], [], []
    sc_l, sn_l, sm_l, ssc_l, sfc_l = [], [], [], [], []
    for l in range(DEPTH):
        xp, c, n, m, sc, fc = block(
            xp,
            jnp.zeros((bsz, N_HEADS, DK, DV), jnp.float32),
            jnp.zeros((bsz, N_HEADS, DK), jnp.float32),
            jnp.zeros((bsz, N_HEADS), jnp.float32),
            jnp.zeros((bsz, CONV_W - 1, D_CONV), xp.dtype),
            jnp.zeros((bsz, CONV_W - 1, 2 * D_FF), xp.dtype),
            N_META, norm1_g[l], w_in[l], b_if[l], w_shortconv[l], w_out[l],
            norm2_g[l], w_up[l], w_ffconv[l], w_down[l])
        pc.append(c); pn.append(n); pm.append(m); psc.append(sc); pfc.append(fc)
        xs, c, n, m, sc, fc = block(
            xs, state_mlstm_C[l], state_mlstm_n[l], state_mlstm_m[l], state_shortconv[l],
            state_ffnconv[l], xs.shape[1], norm1_g[l], w_in[l], b_if[l], w_shortconv[l],
            w_out[l], norm2_g[l], w_up[l], w_ffconv[l], w_down[l])
        sc_l.append(c); sn_l.append(n); sm_l.append(m); ssc_l.append(sc); sfc_l.append(fc)
    y_prompt = rmsnorm(xp, norm_f_g)[:, N_META:]
    y_sample = rmsnorm(xs, norm_f_g)
    return (y_prompt, y_sample,
            jnp.stack(pc), jnp.stack(pn), jnp.stack(pm), jnp.stack(psc), jnp.stack(pfc),
            jnp.stack(sc_l), jnp.stack(sn_l), jnp.stack(sm_l), jnp.stack(ssc_l), jnp.stack(sfc_l))


_drawn_inputs = setup_inputs


def setup_inputs(seed=0):
    import zlib

    import numpy as np

    out = dict(_drawn_inputs(seed))
    spreads = {}
    factors = {'norm2_g': 2.904, 'norm_f_g': 2.826}
    for name, (base, spread) in spreads.items():
        noise = np.random.default_rng([zlib.crc32(name.encode()), seed]).standard_normal(out[name].shape)
        drawn = base * np.exp(spread * noise) if base else spread * noise
        out[name] = __import__('jax').numpy.asarray(drawn.astype(out[name].dtype))
    for name, factor in factors.items():
        out[name] = (out[name] * factor).astype(out[name].dtype)
    return out
```

```python
import numpy as np
import concourse.bass as bass
from concourse import mybir
from contextlib import ExitStack


def hybrid_decoder_step(nc, ins, outs, scratch_rows, scratch_v):
    f32, f32r = mybir.dt.float32, mybir.dt.float32r
    ALU, ACT = mybir.AluOpType, mybir.ActivationFunctionType

    (x_prompt, x_sample, state_C, state_n, state_m, state_sconv, state_fconv, meta, norm1_g,
     w_in, b_if, w_sconv, w_out, norm2_g, w_up, w_fconv, w_down, norm_f_g) = ins
    (y_prompt, y_sample, p_C, p_n, p_m, p_sconv, p_fconv,
     s_C, s_n, s_m, s_sconv, s_fconv) = outs

    P = 128
    D = w_in.shape[1]
    NMETA = meta.shape[0]
    SEQ = x_prompt.shape[1]
    NS = x_sample.shape[0]
    H = state_C.shape[2]
    DK, DV = state_C.shape[3], state_C.shape[4]
    DFF = w_down.shape[1]
    EPS = 1e-6
    KSCALE = DK ** -0.5
    KT = D // P
    FT = DFF // P
    TP = NMETA + SEQ
    NT = TP + NS
    CW = w_sconv.shape[1]
    C0 = NMETA - 2 * (CW - 1)
    M0 = NMETA - (CW - 1)
    NC_ = NT - C0
    NM = NT - M0
    PM = TP - M0
    NF = NT - NMETA
    T2 = TP - 2 * P
    TL = NT - 2 * P
    NLAST = CW - 1 + NS
    OU, OC, OB = 0, D, 2 * D
    OQ = 3 * D
    OK = OQ + H * DK
    OV = OK + H * DK
    OO = OV + H * DV
    OIF = OO + H * DV
    OGA = OIF + 2 * H
    OGB = OGA + D

    KU = 8
    RING = 4
    HST = 15
    CH = 2
    FC = FT // CH
    DOWN_UNITS = ((0, 8), (8, 8), (16, FC - 16))
    HEAD_U = 32
    U_B = H * HEAD_U
    U_C = U_B + 2 * KT
    U_CH = 4 * FC + 3 * KT
    S_B = U_B // 2
    S_C = S_B + KT
    S_CH = 2 * FC + KT
    U_END = U_C + CH * U_CH
    R_EM, R_DEC, R_W, R_ES, RW = PM, 2 * PM, 2 * PM + NS, 2 * PM + 2 * NS, 2 * PM + 3 * NS
    Q1, Q2 = P - M0, 2 * P - M0
    W1 = PM
    W2 = W1 + PM - Q1
    WG = W2 + T2
    WN = WG + 3

    ctx = ExitStack()
    with ctx:
        def sb(name, shape, dt=f32):
            return ctx.enter_context(nc.sbuf_tensor(name, shape, dt))

        def sem(name):
            return ctx.enter_context(nc.semaphore(name))

        xres = sb("xres", [P, KT, NT])
        xh = sb("xh", [P, KT, NT], f32r)
        xl = sb("xl", [P, KT, NT], f32r)
        w_raw = sb("w_raw", [P, RING, KU * P])
        w_hi = sb("w_hi", [P, RING, KU * P], f32r)
        w_lo = sb("w_lo", [P, RING, KU * P], f32r)
        ident = sb("ident", [P, P])
        ones = sb("ones", [P, P])
        vecs = sb("vecs", [P, 6 * KT + CW * 2 * FT])
        rbc = sb("rbc", [P, NT])
        pre_s = sb("pre_s", [P, KT, NS])
        pre_f = sb("pre_f", [P, 2 * FT, NS])
        n_new = sb("n_new", [P, NS, H])
        pn_new = sb("pn_new", [P, H])
        cu_last = sb("cu_last", [P, NLAST, KT])
        up_last = sb("up_last", [P, NLAST, 2 * FT])
        acc = sb("acc", [P, NM])
        scn = sb("scn", [P, 2 * P + NS * H])
        a3 = sb("a3", [P, 3, H])
        scale_t = sb("scale_t", [P, NS])

        base = (nc.sbuf_base + 31) // 32 * 32
        REGION = (nc.sbuf_usable_end - base - 64) // 32 * 32
        sb("region", [P, REGION // 4])
        cursor = [0]

        def at(name, shape, dt=f32):
            size = int(np.prod(shape[1:])) * 4
            size = (size + 31) // 32 * 32
            t = nc.alloc_sbuf_tensor_at(name, shape, dt, offset=base + cursor[0])
            cursor[0] += size
            assert cursor[0] <= REGION, (name, cursor[0])
            return t

        mh = at("mh", [P, KT, NM], f32r)
        ml = at("ml", [P, KT, NM], f32r)
        c_st = at("c_st", [P, NS, DV])
        vb = at("vb", [P, NS, DV])
        q_t = at("q_t", [P, NM])
        k_t = at("k_t", [P, NT])
        v_t = at("v_t", [P, 2, NT])
        v_tok = at("v_tok", [P, 3, DV + 1])
        kg = at("kg", [P, 3, DK])
        arg = at("arg", [P, WN])
        wx = at("wx", [P, WN])
        mask = at("mask", [P, WN])
        pt = at("pt", [P, WG])
        rb = at("rb", [P, RW])
        den = at("den", [P, NM])
        rden = at("rden", [P, NM])
        h_t = at("h_t", [P, 2, NM])
        pc = at("pc", [P, DV + 1])
        vs = at("vs", [NS, DV])
        us = at("us", [P, NC_])
        cgs = at("cgs", [P, NC_])
        cu = at("cu", [P, NC_])
        cv = at("cv", [P, NM])
        bs = at("bs", [P, NM])
        ga = at("ga", [P, NM])
        go = at("go", [P, NM])
        gb = at("gb", [P, NM])
        sa = at("sa", [P, NM])
        so = at("so", [P, NM])
        sbm = at("sbm", [P, NM])
        at_ = at("at_", [P, NM])
        mx = at("mx", [P, NM])
        g3 = at("g3", [P, 3])
        wsc = at("wsc", [P, NS])
        kw = at("kw", [P, NS])
        qp = at("qp", [P, 2 * NS])
        sn = at("sn", [P, NS])
        s_s = at("s_s", [P, NS])
        dq = at("dq", [P, NS])
        num_s = at("num_s", [P, 2, NS])
        sv = at("sv", [P, 2, NS])
        cursor[0] = 0
        x_tok = at("x_tok", [P, 3, D])
        var_rows = at("var_rows", [6 * KT, P])
        wf_rows = at("wf_rows", [2 * FT, CW, P])
        sc_rows = at("sc_rows", [P, 2, P])
        n_rows = at("n_rows", [NS * H, P])
        gw = at("gw", [P, KT, 2 * H])
        gwg = at("gwg", [P, KT, 2 * H])
        b_row = at("b_row", [P, 2 * H])
        ssq = at("ssq", [P, 3])
        rms = at("rms", [P, 3])
        msq = at("msq", [P, 3])
        rtok = at("rtok", [P, 3])
        assert cursor[0] <= 2 * KT * NM * 4
        cursor[0] = 2 * KT * NM * 4
        fc_rows = at("fc_rows", [P, 11, P])
        fct = at("fct", [P, NS, CW - 1, 2 * FT])
        tmp_f = at("tmp_f", [P, 2 * FT, NS])
        assert cursor[0] <= 2 * KT * NM * 4 + 2 * NS * DV * 4
        cursor[0] = 2 * KT * NM * 4 + 2 * NS * DV * 4 + 22 * 1024
        sq_junk = at("sq_junk", [P, D])
        cursor[0] = 2 * KT * NM * 4 + 2 * NS * DV * 4 + 30 * 1024
        diag = at("diag", [P, 3, P])
        gz = at("gz", [P, 3, 2 * H])
        gabs = at("gabs", [P, 3, H])
        gex = at("gex", [P, 3, H])
        gln = at("gln", [P, 3, H])
        lft = at("lft", [P, 3, H])
        lf = at("lf", [H, NT])
        ig = at("ig", [H, NT])
        bcum = at("bcum", [H, TP])
        aa = at("aa", [H, TP])
        mm_ = at("mm_", [H, TP])
        mt = at("mt", [H, TP])
        ex = at("ex", [H, PM + 3 * NS])
        rows = at("rows", [H, RW])
        mp = at("mp", [H, NS])
        t1 = at("t1", [H, NS])
        ms_ = at("ms_", [H, NS])
        ones_row = at("ones_row", [H, TP])
        cursor[0] = 2 * KT * NM * 4
        x2s = at("x2s", [P, NM])
        sqs = at("sqs", [P, NM])
        cursor_co = cursor[0]
        co = at("co", [KT, NLAST, P])
        no = at("no", [NS * H, P])
        pno = at("pno", [H, P])
        rm2 = at("rm2", [P, NM])
        rt2 = at("rt2", [P, NM])
        zs = at("zs", [P, 2, NM])
        cz = at("cz", [P, 2, NF])
        sg = at("sg", [P, NF])
        gg = at("gg", [P, NF])
        hid = at("hid", [P, NF])
        x3 = at("x3", [P, 2, NF])
        xg3 = at("xg3", [P, 2, NF])
        rf = at("rf", [P, 3])
        rfm = at("rfm", [P, 3])
        rfr = at("rfr", [P, 3])
        hh_b = cursor[0]
        cursor[0] = 0
        hl = at("hl", [P, FC, NF], f32r)
        cursor[0] = hh_b
        hh = at("hh", [P, FC, NF], f32r)
        yt = at("yt", [P, 2, D])
        cursor[0] = FC * NF * 4
        ys = at("ys", [NS, D])
        cursor[0] = cursor_co
        uo = at("uo", [2 * FT, NLAST, P])

        bank = [ctx.enter_context(nc.psum_tensor(f"strip{i}", [P, 512], f32)) for i in range(RING)]
        aux = [ctx.enter_context(nc.psum_tensor(f"aux{i}", [P, 512], f32)) for i in range(4)]

        unit_landed = [sem(f"unit_landed{i}") for i in range(RING)]
        hi_done = sem("hi_done")
        lo_done = sem("lo_done")
        unit_used = sem("unit_used")
        evacuated = sem("evacuated")
        params_in, states_in, gates_in = sem("params_in"), sem("states_in"), sem("gates_in")
        x_in = [sem("x_in0"), sem("x_in1")]
        fconv_in = sem("fconv_in")
        const_done = sem("const_done")
        params_turned, copied = sem("params_turned"), sem("copied")
        x_turned, x_copied, xh_done, xl_done = sem("x_turned"), sem("x_copied"), sem("xh_done"), sem("xl_done")
        gw_scaled, gz_done = sem("gw_scaled"), sem("gz_done")
        ssq_done, ms_done, rms_done, rtok_done, diag_done = (
            sem("ssq_done"), sem("ms_done"), sem("rms_done"), sem("rtok_done"), sem("diag_done"))
        r_spread, r_done = sem("r_spread"), sem("r_done")
        f_turned, g_step, g_act = sem("f_turned"), sem("g_step"), sem("g_act")
        g_turned, s_step, a_turned, a3_done = sem("g_turned"), sem("s_step"), sem("a_turned"), sem("a3_done")
        rows_done, rows_stored, rb_in = sem("rows_done"), sem("rows_stored"), sem("rb_in")
        pre_step = sem("pre_step")
        c_in, c_stored, vs_stored, vb_in, pc_stored = (
            sem("c_in"), sem("c_stored"), sem("vs_stored"), sem("vb_in"), sem("pc_stored"))
        arg_done, exp_done, masked, g3_done, p_done = (
            sem("arg_done"), sem("exp_done"), sem("masked"), sem("g3_done"), sem("p_done"))
        scores_done, kv_turned, kv_done, vs_done = (
            sem("scores_done"), sem("kv_turned"), sem("kv_done"), sem("vs_done"))
        wsc_done, kw_done, qk_done, qn_done, sn_done = (
            sem("wsc_done"), sem("kw_done"), sem("qk_done"), sem("qn_done"), sem("sn_done"))
        sample_done, num_done, cn_done, pc_done = (
            sem("sample_done"), sem("num_done"), sem("cn_done"), sem("pc_done"))
        h_step, n_step = sem("h_step"), sem("n_step")
        vk_done, dec_done, c_updated = sem("vk_done"), sem("dec_done"), sem("c_updated")
        cu_done, conv_step, a_done, ag_done, p_gate, b_done, mixed, mix_split = (
            sem("cu_done"), sem("conv_step"), sem("a_done"), sem("ag_done"), sem("p_gate"),
            sem("b_done"), sem("mixed"), sem("mix_split"))
        sig_a, sig_o, sig_b = sem("sig_a"), sem("sig_o"), sem("sig_b")
        sq_done, acc_done, x2g_step, acc_clear = (
            sem("sq_done"), sem("acc_done"), sem("x2g_step"), sem("acc_clear"))
        last_turned, last_copied, r2_spread, r2_step, r2_root = (
            sem("last_turned"), sem("last_copied"), sem("r2_spread"), sem("r2_step"), sem("r2_root"))
        fconv_step, sig_f, gg_done, hid_done, hid_split = (
            sem("fconv_step"), sem("sig_f"), sem("gg_done"), sem("hid_done"), sem("hid_split"))
        x3_step, y_turned, y_copied, ssqf_done, rf_step, rf_root, y_done = (
            sem("x3_step"), sem("y_turned"), sem("y_copied"), sem("ssqf_done"), sem("rf_step"),
            sem("rf_root"), sem("y_done"))
        up_turned, up_copied = sem("up_turned"), sem("up_copied")
        last_stored, moved, stored = sem("last_stored"), sem("moved"), sem("stored")

        block = ctx.enter_context(nc.Block())

        def used(u):
            return u + 1 + RING

        def out_of(s):
            return s + 1 + RING

        def col(c, j):
            return vecs[:, bass.ds(c * KT + j, 1)]

        @block.sync
        def _(sp):
            x_t = [(0, 0, NMETA, meta), (0, NMETA, P, x_prompt[0, 0:P - NMETA, :]),
                   (1, 0, P, x_prompt[0, P - NMETA:2 * P - NMETA, :]),
                   (2, 0, T2, x_prompt[0, 2 * P - NMETA:SEQ, :]),
                   (2, T2, TL, x_sample[:, 0, :])]
            for h in range(2):
                for j, a, b, src in x_t:
                    c = slice(h * D // 2, (h + 1) * D // 2)
                    sp.dma_start(x_tok[a:b, j, c], src[:, c]).then_inc(x_in[h], 16)
            sp.sem_inc(lo_done, RING)

            def load(u, slot, src, kk):
                sp.wait_ge(lo_done, u + 1)
                sp.dma_start(w_raw[:, slot, 0:kk * P].rearrange("p (k n) -> p k n", k=kk),
                             src).then_inc(unit_landed[slot], 16)

            w_in_v = w_in[0].rearrange("(k p) n -> p k n", p=P)
            w_out_v = w_out[0].rearrange("(k p) n -> p k n", p=P)
            w_up_v = w_up[0].rearrange("(k p) n -> p k n", p=P)
            w_down_v = w_down[0].rearrange("(k p) n -> p k n", p=P)

            def load_strip(u, i, view, c):
                for h in range(2):
                    load(u + h, (i + h) % RING, view[:, h * KU:(h + 1) * KU, bass.ds(c, P)], KU)

            def front(n):
                for s, c in enumerate((OQ + n * DK, OK + n * DK, OV + n * DV, OV + n * DV + P)):
                    load_strip(n * HEAD_U + 2 * s, 2 * s, w_in_v, c)

            def back(n):
                for jj in range(2):
                    for s, o in enumerate((OU, OC, OB, OGA, OO, OGB)):
                        load_strip(n * HEAD_U + 8 + 12 * jj + 2 * s, 2 * s, w_in_v, n * DV + o + jj * P)

            front(0)
            with sp.Fori(0, H - 1) as n:
                back(n)
                front(n + 1)
            back(H - 1)
            with sp.Fori(0, KT // 4) as i:
                for q in range(4):
                    load_strip(i * 8 + (U_B + 2 * q), 2 * q, w_out_v, i * (4 * P) + q * P)
            for c in range(CH):
                u0 = U_C + c * U_CH
                with sp.Fori(1, FC // 2 + 1) as i:
                    for p in range(2):
                        f = i * (2 * P) + (c * FC + p - 2) * P
                        load_strip(i * 8 + (u0 + 4 * p - 8), 0, w_up_v, f + DFF)
                        load_strip(i * 8 + (u0 + 4 * p - 6), 2, w_up_v, f)
                u1 = u0 + 4 * FC
                with sp.Fori(0, KT // 4) as i:
                    for q in range(4):
                        for h, (k, kk) in enumerate(DOWN_UNITS):
                            load(i * 12 + (u1 + 3 * q + h), (3 * q + h) % RING,
                                 w_down_v[:, c * FC + k:c * FC + k + kk, bass.ds(i * (4 * P) + q * P, P)], kk)
            sp.wait_ge(y_done, 1)
            sp.dma_start(y_prompt[0, 0:P, :], yt[:, 0, :]).then_inc(stored, 16)
            sp.wait_ge(y_done, 2)
            sp.dma_start(y_sample[:, 0, :], ys[:, :]).then_inc(stored, 16)

        @block.gpsimd
        def _(g):
            g.memset(ident[:, :], 0.0).then_inc(const_done, 1)
            g.memset(ones[:, :], 1.0).then_inc(const_done, 1)
            g.wait_ge(const_done, 2)
            g.affine_select(out=ident[:, :], in_=ident[:, :], compare_op=ALU.not_equal, fill=1.0,
                            base=0, pattern=[[-1, P]], channel_multiplier=1).then_inc(const_done, 1)
            vr = [(norm1_g[0], 0, 1), (norm2_g[0], 1, 1), (norm_f_g, 2, 1)]
            for src, c, _ in vr:
                g.dma_start(var_rows[c * KT:(c + 1) * KT, :], src.rearrange("(j p) -> j p", p=P)).then_inc(params_in, 16)
            g.dma_start(var_rows[3 * KT:6 * KT, :], w_sconv[0].rearrange("c (j p) -> (c j) p", p=P)).then_inc(params_in, 16)
            g.dma_start(wf_rows[:, :, :], w_fconv[0].rearrange("c (f p) -> f c p", p=P)).then_inc(params_in, 16)
            g.dma_start(gw[:, :, :], w_in[0].rearrange("(k p) n -> p k n", p=P)[:, :, OIF:OIF + 2 * H]).then_inc(gates_in, 16)
            g.dma_start(b_row[:, :], b_if.broadcast_to([P, 2 * H])).then_inc(gates_in, 16)
            g.dma_start(sc_rows[:, :, :], state_sconv[0].rearrange("b t (j p) -> (b t j) p", p=P)
                        .rearrange("(h r) p -> r h p", h=2)).then_inc(states_in, 16)
            g.dma_start(n_rows[:, :], state_n[0].rearrange("b h k -> (b h) k")).then_inc(states_in, 16)
            with nc.allow_non_contiguous_dma(reason="64 stabilisers"):
                g.dma_start(mp[:, :], state_m[0].rearrange("b h -> h b")).then_inc(states_in, 16)
            g.dma_start(fc_rows[:, :, :], state_fconv[0].rearrange("b t (f p) -> (b t f) p", p=P)
                        .rearrange("(h r) p -> r h p", r=P)).then_inc(fconv_in, 16)
            g.dma_start(s_sconv[0, :, 0, :], state_sconv[0, :, 1, :]).then_inc(moved, 16)
            g.dma_start(s_fconv[0, :, 0, :], state_fconv[0, :, 1, :]).then_inc(moved, 16)
            g.memset(acc[:, :], 0.0).then_inc(const_done, 1)
            g.memset(gz[:, :, :], 0.0).then_inc(const_done, 1)
            g.memset(a3[:, :, :], 0.0).then_inc(const_done, 1)
            g.memset(ones_row[:, :], 1.0).then_inc(const_done, 1)
            for k in range(KT):
                g.wait_ge(x_copied, k + 1)
                if k == 0:
                    g.wait_ge(copied, 1)
                g.tensor_scalar(xh[:, k, :], xres[:, k, :], vecs[:, k:k + 1], None, ALU.mult).then_inc(xh_done, 1)
                if k == 0:
                    g.wait_ge(gates_in, 32)
                    g.tensor_tensor(gwg[:, :, :], gw[:, :, :], vecs[:, 0:KT].unsqueeze(2).broadcast_to([P, KT, 2 * H]),
                                    ALU.mult).then_inc(gw_scaled, 1)
            g.wait_ge(gz_done, 1)
            g.memset(scale_t[:, :], KSCALE).then_inc(const_done, 1)
            g.memset(mask[:, :], 1.0).then_inc(const_done, 1)
            g.memset(arg[:, :], 0.0).then_inc(const_done, 1)
            g.memset(pt[:, :], 0.0).then_inc(const_done, 1)
            g.memset(v_tok[:, 0:2, :], 1.0).then_inc(const_done, 1)
            g.memset(v_tok[:, 2, :], 0.0).then_inc(const_done, 1)
            g.memset(kg[:, :, :], 0.0).then_inc(const_done, 1)
            g.wait_ge(const_done, 14)
            g.memset(v_tok[0:T2, 2, DV:DV + 1], 1.0).then_inc(const_done, 1)
            for c0, q0, s0, rows_, nq in ((0, M0, 0, P, PM), (W1, P, P, P, PM - Q1), (W2, 2 * P, 2 * P, T2, T2)):
                g.affine_select(out=mask[0:rows_, c0:c0 + nq], in_=mask[0:rows_, c0:c0 + nq], compare_op=ALU.is_ge,
                                fill=0.0, base=q0 - s0, pattern=[[1, nq]], channel_multiplier=-1)\
                 .then_inc(const_done, 1)
            scv = scn[:, 0:2 * P].rearrange("p (b t j) -> p t j b", b=NS, t=CW - 1)
            g.wait_ge(copied, 5)

            def spread(lo, n):
                return vecs[:, lo:lo + n].unsqueeze(2).broadcast_to([P, n, NS])

            ts = tmp_f[:, 0:KT, :]
            g.tensor_tensor(pre_s[:, :, :], scv[:, 0], spread(3 * KT, KT), ALU.mult).then_inc(pre_step, 1)
            g.tensor_tensor(ts, scv[:, 1], spread(4 * KT, KT), ALU.mult).then_inc(pre_step, 1)
            g.wait_ge(pre_step, 2)
            g.tensor_tensor(pre_s[:, :, :], pre_s[:, :, :], ts, ALU.add).then_inc(pre_step, 1)
            fcv = fct[:, :, :, :].rearrange("p b t f -> p t f b")
            g.tensor_tensor(pre_f[:, :, :], fcv[:, 0], spread(6 * KT, 2 * FT), ALU.mult).then_inc(pre_step, 1)
            g.wait_ge(pre_step, 3)
            g.tensor_tensor(tmp_f[:, :, :], fcv[:, 1], spread(6 * KT + 2 * FT, 2 * FT), ALU.mult).then_inc(pre_step, 1)
            g.wait_ge(pre_step, 5)
            g.tensor_tensor(pre_f[:, :, :], pre_f[:, :, :], tmp_f[:, :, :], ALU.add).then_inc(pre_step, 1)

            dec = rb[:, R_DEC:R_DEC + NS]

            def back(n):
                s0 = n * 16
                j0 = n * 2
                g.wait_ge(rb_in, n * 16 + 16)
                g.tensor_tensor(wsc[:, :], rb[:, R_W:R_W + NS], scale_t[:, :], ALU.mult).then_inc(wsc_done, 1)
                g.wait_ge(evacuated, out_of(s0 + 1))
                g.tensor_tensor(qp[:, 0:NS], q_t[:, PM:NM], k_t[:, TP:NT], ALU.mult).then_inc(qk_done, 1)
                g.wait_ge(wsc_done, n + 1)
                g.tensor_tensor(kw[:, :], k_t[:, TP:NT], wsc[:, :], ALU.mult).then_inc(kw_done, 1)
                g.wait_ge(exp_done, n + 1)
                g.tensor_tensor(g3[:, :], wx[:, WG:WN], scale_t[:, 0:3], ALU.mult).then_inc(g3_done, 1)
                g.tensor_tensor(wx[:, 0:WG], wx[:, 0:WG], mask[:, 0:WG], ALU.mult).then_inc(masked, 1)
                for jj in range(2):
                    j = j0 + jj
                    s = s0 + 4 + 6 * jj
                    g.wait_ge(evacuated, out_of(s + 1))
                    g.tensor_tensor(cu[:, :], us[:, :], cgs[:, :], ALU.mult).then_inc(cu_done, 1)
                    g.wait_ge(evacuated, out_of(s + 2))
                    g.wait_ge(conv_step, j * 5 + 5)
                    g.tensor_tensor(at_[:, :], bs[:, :], cv[:, :], ALU.mult).then_inc(a_done, 1)
                    if jj == 0:
                        g.wait_ge(vb_in, n * 16 + 16)
                        g.wait_ge(kw_done, n + 1)
                        g.tensor_tensor(vb[:, :, :], vb[:, :, :], kw[:, :].unsqueeze(2).broadcast_to([P, NS, DV]),
                                        ALU.mult).then_inc(vk_done, 1)
                        g.wait_ge(sample_done, n + 1)
                        g.tensor_tensor(c_st[:, :, :], c_st[:, :, :], dec.unsqueeze(2).broadcast_to([P, NS, DV]),
                                        ALU.mult).then_inc(dec_done, 1)
                        g.wait_ge(vk_done, n + 1)
                        g.wait_ge(dec_done, n + 1)
                        g.tensor_tensor(c_st[:, :, :], c_st[:, :, :], vb[:, :, :], ALU.add).then_inc(c_updated, 1)
                    g.wait_ge(a_done, j + 1)
                    g.wait_ge(sig_a, j + 1)
                    g.tensor_tensor(at_[:, :], at_[:, :], sa[:, :], ALU.mult).then_inc(ag_done, 1)
                    g.wait_ge(sig_o, j + 1)
                    g.wait_ge(sig_b, j + 1)
                    g.tensor_tensor(so[:, :], so[:, :], sbm[:, :], ALU.mult).then_inc(p_gate, 1)
                    g.wait_ge(p_gate, j + 1)
                    g.wait_ge(h_step, n * HST + HST)
                    g.tensor_tensor(so[:, :], so[:, :], h_t[:, jj, :], ALU.mult).then_inc(b_done, 1)
                    g.wait_ge(ag_done, j + 1)
                    g.wait_ge(b_done, j + 1)
                    g.tensor_tensor(mx[:, :], at_[:, :], so[:, :], ALU.add).then_inc(mixed, 1)

            back(0)
            with g.Fori(1, H) as n:
                back(n)
            g.sem_inc(acc_done, 1)
            with g.Fori(0, KT) as m:
                g.wait_ge(sq_done, m + 2)
                g.wait_ge(acc_done, m + 1)
                g.tensor_tensor(acc[:, :], acc[:, :], sqs[:, :], ALU.add).then_inc(acc_done, 1)
            g.wait_ge(r2_spread, 1)
            g.memset(acc[:, :], 0.0).then_inc(acc_clear, 1)
            with g.Fori(0, FT) as f:
                g.wait_ge(sig_f, f + 1)
                g.tensor_tensor(gg[:, :], sg[:, :], cz[:, 0, :], ALU.mult).then_inc(gg_done, 1)
                g.wait_ge(fconv_step, f * 10 + 10)
                g.wait_ge(gg_done, f + 1)
                g.tensor_tensor(hid[:, :], gg[:, :], cz[:, 1, :], ALU.mult).then_inc(hid_done, 1)
            g.wait_ge(acc_clear, 1)
            with g.Fori(KT, 2 * KT) as m:
                g.wait_ge(sq_done, m + 2)
                g.wait_ge(acc_done, m + 1)
                g.tensor_tensor(acc[:, 0:NF], acc[:, 0:NF], sqs[:, 0:NF], ALU.add).then_inc(acc_done, 1)

        @block.scalar
        def _(act):
            def split_hi(u, slot, n16):
                act.wait_ge(unit_landed[slot], n16)
                act.wait_ge(unit_used, u + 1)
                act.activation(w_hi[:, slot, :], w_raw[:, slot, :], ACT.Copy).then_inc(hi_done, 1)

            def ahead(u0, i):
                slot = i % RING
                turn = u0 // RING + i // RING + 1 if isinstance(u0, int) else None
                return slot, turn

            def step(n, per, base_u, i):
                u4 = n * per + (base_u + i + RING)
                split_hi(u4, i % RING, n * (16 * per // RING) + 16 * ((base_u + i) // RING + 2))

            act.wait_ge(params_turned, 1)
            act.activation(vecs[:, :], aux[0][:, 0:6 * KT + CW * 2 * FT], ACT.Copy).then_inc(copied, 1)
            for k in range(KT):
                act.wait_ge(x_turned, k + 1)
                act.activation(xres[:, k, :], bank[k % RING][:, 0:NT], ACT.Copy).then_inc(x_copied, 1)

            def squares(j):
                r = P if j < 2 else TL
                if j > 0:
                    act.wait_ge(ssq_done, j)
                act.activation(sq_junk[0:r, :], x_tok[0:r, j, :], ACT.Square, accum_out=ssq[0:r, j:j + 1]).then_inc(ssq_done, 1)

            act.wait_ge(x_in[0], 16 * 5)
            act.wait_ge(x_in[1], 16 * 5)
            split_hi(0, 0, 16)
            split_hi(1, 1, 16)
            squares(0)
            split_hi(2, 2, 16)
            squares(1)
            split_hi(3, 3, 16)
            squares(2)
            act.wait_ge(ms_done, 2)
            act.activation(rms[:, 0:2], msq[:, 0:2], ACT.Sqrt).then_inc(rms_done, 1)
            act.activation(rms[0:TL, 2:3], msq[0:TL, 2:3], ACT.Sqrt).then_inc(rms_done, 1)

            def front(n, first=False):
                for i in range(8):
                    step(n, HEAD_U, 0, i)
                    if first and i == 0:
                        act.wait_ge(g_step, 4)
                        act.activation(gex[:, :, :], gabs[:, :, :], ACT.Exp).then_inc(g_act, 1)
                    if first and i == 2:
                        act.wait_ge(g_step, 5)
                        act.activation(gln[:, :, :], gex[:, :, :], ACT.Ln).then_inc(g_act, 1)
                        for t in range(2):
                            act.wait_ge(f_turned, 1 + t)
                            act.activation(fct[:, :, :, :].rearrange("p b t f -> p (b t f)")[:, 512 * t:512 * t + 512],
                                           aux[2 + t][:, :], ACT.Copy).then_inc(copied, 1)
                    if first and i == 4:
                        act.wait_ge(f_turned, 3)
                        act.activation(fct[:, :, :, :].rearrange("p b t f -> p (b t f)")[:, 1024:11 * P],
                                       aux[0][:, 0:3 * P], ACT.Copy).then_inc(copied, 1)
                        act.wait_ge(f_turned, 4)
                        act.activation(scn[:, :], aux[2][:, 0:2 * P + NS * H], ACT.Copy).then_inc(copied, 1)
                    if first and i == 6:
                        act.wait_ge(s_step, 13)
                        act.activation(rows[:, R_EM:RW], ex[:, :], ACT.Exp).then_inc(rows_done, 1)
                        act.wait_ge(rows_done, 1)
                        act.dma_start(scratch_rows, rows[:, :]).then_inc(rows_stored, 16)
                        act.dma_start(p_m.rearrange("a b h -> h (a b)"), mt[:, TP - 1:TP]).then_inc(rows_stored, 16)
                        with nc.allow_non_contiguous_dma(reason="64 stabilisers"):
                            act.dma_start(s_m[0].rearrange("b h -> h b"), ms_[:, :]).then_inc(rows_stored, 16)
                        act.wait_ge(rows_stored, 48)
                    if i == 7:
                        if not first:
                            act.wait_ge(h_step, n * HST)
                            act.wait_ge(n_step, n * 2)
                            act.wait_ge(c_updated, n)
                            act.wait_ge(c_stored, n * 16)
                            act.wait_ge(pc_stored, n * 16)
                        else:
                            act.wait_ge(pre_step, 6)
                        act.dma_start(rb[:, :], scratch_rows[bass.ds(n, 1), :].broadcast_to([P, RW])).then_inc(rb_in, 16)
                        act.dma_start(c_st[:, :, :], state_C[0].rearrange("b h k v -> h k b v")[n]).then_inc(c_in, 16)

            def back(n):
                j0 = n * 2
                s0 = n * 16
                for i in range(8, HEAD_U):
                    step(n, HEAD_U, 0, i)
                    if i == 8:
                        act.wait_ge(arg_done, n + 1)
                        act.activation(wx[:, :], arg[:, :], ACT.Exp).then_inc(exp_done, 1)
                    if i == 10:
                        act.wait_ge(kv_turned, n + 1)
                        act.wait_ge(g3_done, n + 1)
                        act.activation(vs[:, :], aux[3][0:NS, P:P + DV], ACT.Copy).then_inc(vs_done, 1)
                        act.activation(v_tok[:, 0:2, 0:DV], aux[1][:, :].rearrange("p (j v) -> p j v", j=2), ACT.Copy)
                        for t in range(2):
                            act.activation(kg[:, t, :], aux[2][:, t * P:(t + 1) * P], ACT.Copy, scale=g3[:, t:t + 1])
                        act.activation(v_tok[0:T2, 2, 0:DV], aux[2][0:T2, 2 * P:2 * P + DV], ACT.Copy)
                        act.activation(kg[0:T2, 2, :], aux[3][0:T2, 0:P], ACT.Copy, scale=g3[0:T2, 2:3]).then_inc(kv_done, 1)
                        act.wait_ge(vs_done, n + 1)
                        act.dma_start(scratch_v[bass.ds(n, 1), :].rearrange("a (b v) -> (a b) v", b=NS), vs[:, :])\
                           .then_inc(vs_stored, 16)
                    if i == 11:
                        act.wait_ge(vs_stored, n * 16 + 16)
                        act.dma_start(vb[:, :, :].rearrange("p b v -> p (b v)"),
                                      scratch_v[bass.ds(n, 1), :].broadcast_to([P, NS * DV])).then_inc(vb_in, 16)
                    if i == 14:
                        act.wait_ge(cn_done, n + 1)
                        act.activation(pc[:, :], aux[3][:, 0:DV + 1], ACT.Copy).then_inc(pc_done, 1)
                        act.wait_ge(pc_done, n + 1)
                        act.dma_start(p_C[0, 0].rearrange("h k v -> h k v")[n], pc[:, 0:DV]).then_inc(pc_stored, 16)
                    for jj in range(2):
                        if i == 15 + 12 * jj:
                            act.wait_ge(evacuated, out_of(s0 + 7 + 6 * jj))
                            act.activation(sa[:, :], ga[:, :], ACT.Sigmoid).then_inc(sig_a, 1)
                        if i == 17 + 12 * jj:
                            act.wait_ge(evacuated, out_of(s0 + 8 + 6 * jj))
                            act.activation(so[:, :], go[:, :], ACT.Sigmoid).then_inc(sig_o, 1)
                        if i == 19 + 12 * jj:
                            act.wait_ge(evacuated, out_of(s0 + 9 + 6 * jj))
                            act.activation(sbm[:, :], gb[:, :], ACT.Sigmoid).then_inc(sig_b, 1)
                    if i == 24:
                        act.wait_ge(c_updated, n + 1)
                        act.dma_start(s_C[0].rearrange("b h k v -> h k b v")[n], c_st[:, :, :]).then_inc(c_stored, 16)

            front(0, first=True)
            with act.Fori(0, H - 1) as n:
                back(n)
                front(n + 1)
            back(H - 1)

            def square_into(m, src):
                act.wait_ge(acc_done, m + 1)
                act.activation(sqs[:, 0:src.shape[1]], src, ACT.Square).then_inc(sq_done, 1)

            act.sem_inc(sq_done, 1)
            with act.Fori(0, KT // 4) as n:
                for q in range(4):
                    step(n, 8, U_B, 2 * q)
                    step(n, 8, U_B, 2 * q + 1)
                    act.wait_ge(evacuated, out_of(n * 4 + (S_B + q)))
                    square_into(n * 4 + q, x2s[:, :])
            act.wait_ge(last_turned, 1)
            for t in range(2):
                act.activation(co[:, 4 * t:4 * t + 4, :].rearrange("j t p -> j (t p)"), aux[1 + t][0:KT, :], ACT.Copy)
            act.activation(co[:, 8:10, :].rearrange("j t p -> j (t p)"), aux[3][0:KT, 0:2 * P], ACT.Copy).then_inc(last_copied, 1)
            act.activation(no[:, :], aux[3][0:NS * H, 2 * P:3 * P], ACT.Copy)
            act.activation(pno[:, :], aux[3][0:H, 3 * P:4 * P], ACT.Copy).then_inc(last_copied, 1)
            act.wait_ge(r2_step, 1)
            act.activation(rt2[:, :], rm2[:, :], ACT.Sqrt).then_inc(r2_root, 1)
            act.wait_ge(last_copied, 2)
            for t in range(NLAST):
                dst = p_sconv[0, 0, t, :] if t < CW - 1 else s_sconv[0, t - (CW - 1), CW - 2, :]
                act.dma_start(dst.rearrange("(j p) -> j p", p=P), co[:, t, :]).then_inc(last_stored, 16)
            act.dma_start(s_n[0].rearrange("b h k -> (b h) k"), no[:, :]).then_inc(last_stored, 16)
            act.dma_start(p_n[0, 0], pno[:, :]).then_inc(last_stored, 16)

            for c in range(CH):
                u0 = U_C + c * U_CH
                with act.Fori(0, FC // 2) as n:
                    for p in range(2):
                        step(n, 8, u0, 4 * p)
                        step(n, 8, u0, 4 * p + 1)
                        step(n, 8, u0, 4 * p + 2)
                        act.wait_ge(fconv_step, n * 20 + (10 * c * FC + 10 * p + 5))
                        act.activation(sg[:, :], cz[:, 0, :], ACT.Sigmoid).then_inc(sig_f, 1)
                        step(n, 8, u0, 4 * p + 3)
                u1 = u0 + 4 * FC
                if c == 0:
                    with act.Fori(0, KT // 4) as n:
                        for i in range(12):
                            step(n, 12, u1, i)
            for m in range(KT):
                for i in range(3):
                    if u1 + 3 * m + i + RING < U_END:
                        step(0, 12, u1, 3 * m + i)
                if m == 1:
                    act.wait_ge(last_stored, 16 * (NLAST + 2))
                    for t in range(3):
                        act.wait_ge(up_turned, t + 1)
                        w = min(4, NLAST - 4 * t)
                        act.activation(uo[:, 4 * t:4 * t + w, :].rearrange("f t p -> f (t p)"),
                                       aux[t][0:2 * FT, 0:w * P], ACT.Copy).then_inc(up_copied, 1)
                    act.wait_ge(up_copied, 3)
                    for t in range(NLAST):
                        dst = p_fconv[0, 0, t, :] if t < CW - 1 else s_fconv[0, t - (CW - 1), CW - 2, :]
                        act.dma_start(dst.rearrange("(f p) -> f p", p=P), uo[:, t, :]).then_inc(stored, 16)
                act.wait_ge(x3_step, 2 * m + 1)
                square_into(KT + m, x3[:, m % 2, :])
                if m % 4 == 0 and m > 0:
                    gq = m // 4 - 1
                    act.wait_ge(y_turned, 4 * (gq + 1))
                    for t in range(2):
                        act.activation(yt[:, t, 512 * gq:512 * gq + 512], aux[t][:, :], ACT.Copy).then_inc(y_copied, 1)
                    act.activation(ys[:, 512 * gq:512 * gq + 512], aux[2][0:NS, :], ACT.Copy).then_inc(y_copied, 1)
            gq = KT // 4 - 1
            act.wait_ge(y_turned, KT)
            for t in range(2):
                act.activation(yt[:, t, 512 * gq:512 * gq + 512], aux[t][:, :], ACT.Copy).then_inc(y_copied, 1)
            act.activation(ys[:, 512 * gq:512 * gq + 512], aux[2][0:NS, :], ACT.Copy).then_inc(y_copied, 1)
            act.wait_ge(rf_step, 2)
            act.activation(rfr[:, 0:2], rfm[:, 0:2], ACT.Sqrt).then_inc(rf_root, 1)
            act.activation(rfr[0:NS, 2:3], rfm[0:NS, 2:3], ACT.Sqrt).then_inc(rf_root, 1)
            act.wait_ge(rf_step, 12)
            act.wait_ge(y_copied, 3 * KT // 4)
            act.activation(yt[:, 1, :], yt[:, 1, :], ACT.Copy, scale=rf[:, 1:2]).then_inc(rf_root, 1)
            act.wait_ge(rf_root, 3)
            act.dma_start(y_prompt[0, P:2 * P, :], yt[:, 1, :]).then_inc(stored, 16)
            act.wait_ge(pc_stored, 16 * H)
            act.wait_ge(c_stored, 16 * H)
            act.wait_ge(moved, 16 * 2)
            act.wait_ge(stored, 16 * (NLAST + 3))

        @block.vector
        def _(v):
            def split_lo(u, slot):
                v.wait_ge(hi_done, u + 1)
                v.tensor_tensor(w_lo[:, slot, :], w_raw[:, slot, :], w_hi[:, slot, :].bitcast(f32),
                                ALU.subtract).then_inc(lo_done, 1)

            def step(n, per, base_u, i):
                split_lo(n * per + (base_u + i + RING), i % RING)

            def take(u, s, b, out, c0, width):
                v.wait_ge(unit_used, used(u))
                v.tensor_tensor(out, bank[b][:, 0:width], rbc[:, c0:c0 + width], ALU.mult).then_inc(evacuated, 1)

            def refine(r, c, root, mean, out, done, d0):
                v.reciprocal(out[0:r, c], root[0:r, c]).then_inc(done, 1)
                v.wait_ge(done, d0 + 1)
                v.tensor_tensor(root[0:r, c], out[0:r, c], out[0:r, c], ALU.mult).then_inc(done, 1)
                v.wait_ge(done, d0 + 2)
                v.scalar_tensor_tensor(out=root[0:r, c], in0=root[0:r, c], scalar=-0.5, in1=mean[0:r, c],
                                       op0=ALU.mult, op1=ALU.mult).then_inc(done, 1)
                v.wait_ge(done, d0 + 3)
                v.tensor_scalar(root[0:r, c], root[0:r, c], 1.5, None, ALU.add).then_inc(done, 1)
                v.wait_ge(done, d0 + 4)
                v.tensor_tensor(out[0:r, c], out[0:r, c], root[0:r, c], ALU.mult).then_inc(done, 1)

            v.sem_inc(evacuated, RING)
            for k in range(KT):
                v.wait_ge(xh_done, k + 1)
                v.scalar_tensor_tensor(out=xl[:, k, :], in0=xres[:, k, :], scalar=vecs[:, k:k + 1],
                                       in1=xh[:, k, :].bitcast(f32), op0=ALU.mult, op1=ALU.subtract).then_inc(xl_done, 1)
            for u in range(RING):
                split_lo(u, u)
            v.wait_ge(ssq_done, 3)
            v.tensor_scalar(msq[:, 0:2], ssq[:, 0:2], 1.0 / D, EPS, ALU.mult, ALU.add).then_inc(ms_done, 1)
            v.tensor_scalar(msq[0:TL, 2:3], ssq[0:TL, 2:3], 1.0 / D, EPS, ALU.mult, ALU.add).then_inc(ms_done, 1)
            v.wait_ge(rms_done, 2)
            for j, (r, c) in enumerate(((P, slice(0, 2)), (TL, slice(2, 3)))):
                refine(r, c, rms, msq, rtok, rtok_done, 5 * j)
            v.wait_ge(rtok_done, 10)
            for j in range(3):
                r = P if j < 2 else TL
                v.tensor_scalar(diag[0:r, j, :], ident[0:r, :], rtok[0:r, j:j + 1], None, ALU.mult).then_inc(diag_done, 1)
            v.wait_ge(gz_done, 1)
            for j in range(3):
                r = P if j < 2 else TL
                v.scalar_tensor_tensor(out=gz[0:r, j, :], in0=aux[1][0:r, 16 * j:16 * j + 16], scalar=rtok[0:r, j:j + 1],
                                       in1=b_row[0:r, :], op0=ALU.mult, op1=ALU.add).then_inc(g_step, 1)
            v.wait_ge(g_step, 3)
            v.scalar_tensor_tensor(out=gabs[:, :, :], in0=gz[:, :, H:2 * H], scalar=-1.0, in1=gz[:, :, H:2 * H],
                                   op0=ALU.mult, op1=ALU.min).then_inc(g_step, 1)

            def front(n, first=False):
                u0 = n * HEAD_U
                s0 = n * 16
                for i in range(8):
                    step(n, HEAD_U, 0, i)
                    if first and i == 0:
                        v.wait_ge(g_act, 1)
                        v.tensor_scalar(gex[:, :, :], gex[:, :, :], 1.0, None, ALU.add).then_inc(g_step, 1)
                    if first and i == 1:
                        v.wait_ge(r_spread, 1)
                        v.tensor_copy(rbc[:, :], aux[0][:, 0:NT]).then_inc(r_done, 1)
                        v.wait_ge(r_done, 1)
                    if first and i == 2:
                        v.wait_ge(g_act, 2)
                        v.scalar_tensor_tensor(out=lft[:, :, :], in0=gz[:, :, H:2 * H], scalar=0.0, in1=gln[:, :, :],
                                               op0=ALU.min, op1=ALU.subtract).then_inc(g_step, 1)
                    if first and i == 4:
                        v.wait_ge(g_turned, 1)
                        v.tensor_copy(lf[:, :], aux[3][0:H, 0:NT]).then_inc(s_step, 1)
                        v.tensor_copy(ig[:, :], aux[1][0:H, 0:NT]).then_inc(s_step, 1)
                        v.wait_ge(s_step, 1)
                        v.tensor_tensor_scan(bcum[:, :], ones_row[:, :], lf[:, 0:TP], 0.0, ALU.mult, ALU.add).then_inc(s_step, 1)
                        v.wait_ge(s_step, 3)
                        v.tensor_tensor(aa[:, :], ig[:, 0:TP], bcum[:, :], ALU.subtract).then_inc(s_step, 1)
                        v.wait_ge(s_step, 4)
                        v.tensor_tensor_scan(mm_[:, :], ones_row[:, :], aa[:, :], 0.0, ALU.mult, ALU.max).then_inc(s_step, 1)
                        v.wait_ge(states_in, 48)
                        v.tensor_tensor(t1[:, :], lf[:, TP:NT], mp[:, :], ALU.add).then_inc(s_step, 1)
                        v.wait_ge(s_step, 6)
                        v.tensor_scalar(rows[:, 0:PM], mm_[:, M0:TP], -1.0, None, ALU.mult).then_inc(s_step, 1)
                        v.tensor_tensor(mt[:, :], bcum[:, :], mm_[:, :], ALU.add).then_inc(s_step, 1)
                        v.tensor_tensor(ms_[:, :], t1[:, :], ig[:, TP:NT], ALU.max).then_inc(s_step, 1)
                        v.wait_ge(s_step, 9)
                        v.tensor_scalar(ex[:, 0:PM], mt[:, M0:TP], -1.0, None, ALU.mult).then_inc(s_step, 1)
                        v.tensor_tensor(ex[:, PM:PM + NS], t1[:, :], ms_[:, :], ALU.subtract).then_inc(s_step, 1)
                        v.tensor_tensor(ex[:, PM + NS:PM + 2 * NS], ig[:, TP:NT], ms_[:, :], ALU.subtract).then_inc(s_step, 1)
                        v.tensor_scalar(ex[:, PM + 2 * NS:PM + 3 * NS], ms_[:, :], -1.0, None, ALU.mult).then_inc(s_step, 1)
                    if first and i == 6:
                        v.wait_ge(a_turned, 1)
                        v.tensor_copy(a3[:, 0:2, :], aux[3][:, 0:2 * H].rearrange("p (j h) -> p j h", j=2)).then_inc(a3_done, 1)
                        v.tensor_copy(a3[0:T2, 2, :], aux[3][0:T2, 2 * H:3 * H]).then_inc(a3_done, 1)
                        v.wait_ge(a3_done, 2)
                    if i == 1:
                        take(u0 + 1, s0, 0, q_t[:, :], M0, NM)
                    if i == 3:
                        take(u0 + 3, s0 + 1, 1, k_t[:, :], 0, NT)
                    if i == 5:
                        take(u0 + 5, s0 + 2, 2, v_t[:, 0, :], 0, NT)
                    if i == 7:
                        take(u0 + 7, s0 + 3, 3, v_t[:, 1, :], 0, NT)

            dec = rb[:, R_DEC:R_DEC + NS]

            def back(n):
                u0 = n * HEAD_U
                s0 = n * 16
                hs = n * HST
                for i in range(8, HEAD_U):
                    step(n, HEAD_U, 0, i)
                    if i == 8:
                        v.wait_ge(rb_in, n * 16 + 16)
                        for j, (c0, q0, rows_, nq) in enumerate(((0, 0, P, PM), (W1, Q1, P, PM - Q1), (W2, Q2, T2, T2))):
                            v.tensor_scalar(arg[0:rows_, c0:c0 + nq], rb[0:rows_, q0:q0 + nq],
                                            a3[0:rows_, j, bass.ds(n, 1)], 0.0, ALU.add, ALU.min)
                        v.tensor_scalar(arg[:, WG:WN], a3[:, :, bass.ds(n, 1)].rearrange("p j a -> p (j a)"),
                                        rb[:, PM - 1:PM], 0.0, ALU.add, ALU.min).then_inc(arg_done, 1)
                        v.tensor_scalar(sn[:, :], scn[:, 2 * P:].rearrange("p (b h) -> p b h", b=NS)[:, :, bass.ds(n, 1)]
                                        .rearrange("p b a -> p (b a)"), 1.0, None, ALU.mult).then_inc(sn_done, 1)
                        v.wait_ge(sn_done, n + 1)
                        v.tensor_tensor(qp[:, NS:2 * NS], q_t[:, PM:NM], sn[:, :], ALU.mult).then_inc(qn_done, 1)
                    if i == 10:
                        v.wait_ge(scores_done, n + 1)
                        v.wait_ge(masked, n + 1)
                        v.scalar_tensor_tensor(out=pt[:, 0:W2], in0=aux[0][:, 0:W2], scalar=KSCALE, in1=wx[:, 0:W2],
                                               op0=ALU.mult, op1=ALU.mult)
                        v.scalar_tensor_tensor(out=pt[0:T2, W2:WG], in0=aux[0][0:T2, W2:WG], scalar=KSCALE,
                                               in1=wx[0:T2, W2:WG], op0=ALU.mult, op1=ALU.mult).then_inc(p_done, 1)
                    if i == 14:
                        v.wait_ge(num_done, n + 1)
                        v.tensor_tensor(den[:, 0:PM], aux[2][:, 0:PM], rb[:, R_EM:R_EM + PM], ALU.max).then_inc(h_step, 1)
                        v.wait_ge(wsc_done, n + 1)
                        v.tensor_tensor(s_s[:, :], aux[0][:, PM + 2 * NS:PM + 3 * NS], wsc[:, :], ALU.mult).then_inc(h_step, 1)
                        v.tensor_tensor(dq[:, :], aux[0][:, PM + 3 * NS:PM + 4 * NS], dec, ALU.mult).then_inc(h_step, 1)
                        v.tensor_tensor(num_s[:, :, :], aux[0][:, PM:PM + 2 * NS].rearrange("p (a b) -> p a b", a=2),
                                        dec.unsqueeze(1).broadcast_to([P, 2, NS]), ALU.mult).then_inc(h_step, 1)
                        v.wait_ge(h_step, hs + 1)
                        v.scalar_tensor_tensor(out=den[:, 0:PM], in0=aux[2][:, 0:PM], scalar=-1.0, in1=den[:, 0:PM],
                                               op0=ALU.mult, op1=ALU.max).then_inc(h_step, 1)
                        v.wait_ge(h_step, hs + 3)
                        v.tensor_tensor(dq[:, :], dq[:, :], s_s[:, :], ALU.add).then_inc(h_step, 1)
                        v.tensor_tensor(sv[:, :, :], v_t[:, :, TP:NT], s_s[:, :].unsqueeze(1).broadcast_to([P, 2, NS]),
                                        ALU.mult).then_inc(h_step, 1)
                        v.wait_ge(h_step, hs + 6)
                        v.tensor_tensor(den[:, PM:NM], dq[:, :], rb[:, R_ES:R_ES + NS], ALU.max).then_inc(h_step, 1)
                        v.wait_ge(h_step, hs + 8)
                        v.scalar_tensor_tensor(out=den[:, PM:NM], in0=dq[:, :], scalar=-1.0, in1=den[:, PM:NM],
                                               op0=ALU.mult, op1=ALU.max).then_inc(h_step, 1)
                        v.tensor_tensor(num_s[:, :, :], num_s[:, :, :], sv[:, :, :], ALU.add).then_inc(h_step, 1)
                        v.wait_ge(h_step, hs + 9)
                        v.reciprocal(rden[:, :], den[:, :]).then_inc(h_step, 1)
                        v.wait_ge(h_step, hs + 11)
                        v.tensor_tensor(h_t[:, :, PM:NM], num_s[:, :, :], rden[:, PM:NM].unsqueeze(1).broadcast_to([P, 2, NS]),
                                        ALU.mult).then_inc(h_step, 1)
                        v.tensor_tensor(h_t[:, 0, 0:PM], aux[0][:, 0:PM], rden[:, 0:PM], ALU.mult).then_inc(h_step, 1)
                        v.tensor_tensor(h_t[:, 1, 0:PM], aux[1][:, 0:PM], rden[:, 0:PM], ALU.mult).then_inc(h_step, 1)
                        v.tensor_tensor(sn[:, :], sn[:, :], dec, ALU.mult).then_inc(h_step, 1)
                    if i == 16:
                        v.wait_ge(h_step, hs + HST)
                        v.wait_ge(kw_done, n + 1)
                        v.tensor_tensor(n_new[:, :, bass.ds(n, 1)].rearrange("p b a -> p (b a)"), sn[:, :], kw[:, :],
                                        ALU.add).then_inc(n_step, 1)
                        v.wait_ge(pc_done, n + 1)
                        v.tensor_scalar(pn_new[:, bass.ds(n, 1)], pc[:, DV:DV + 1], 1.0, None, ALU.mult).then_inc(n_step, 1)
                    for jj in range(2):
                        j = n * 2 + jj
                        k = i - 12 * jj
                        s = s0 + 4 + 6 * jj
                        if k == 9:
                            take(u0 + i, s, (4 + 6 * jj) % RING, us[:, :], C0, NC_)
                        if k == 11:
                            take(u0 + i, s + 1, (5 + 6 * jj) % RING, cgs[:, :], C0, NC_)
                        if k == 12:
                            v.wait_ge(cu_done, j + 1)
                            v.tensor_scalar(cu_last[:, :, bass.ds(j, 1)].rearrange("p t a -> p (t a)"), cu[:, NC_ - NLAST:NC_],
                                            1.0, None, ALU.mult).then_inc(conv_step, 1)
                            v.tensor_scalar(cv[:, :], cu[:, 2:NC_], col(5, j), None, ALU.mult).then_inc(conv_step, 1)
                            v.wait_ge(conv_step, j * 5 + 2)
                            v.scalar_tensor_tensor(out=cv[:, 0:PM], in0=cu[:, 1:1 + PM], scalar=col(4, j), in1=cv[:, 0:PM],
                                                   op0=ALU.mult, op1=ALU.add).then_inc(conv_step, 1)
                            v.wait_ge(pre_step, 3)
                            v.tensor_tensor(cv[:, PM:NM], cv[:, PM:NM], pre_s[:, bass.ds(j, 1), :].rearrange("p a b -> p (a b)"),
                                            ALU.add).then_inc(conv_step, 1)
                            v.wait_ge(conv_step, j * 5 + 3)
                            v.scalar_tensor_tensor(out=cv[:, 0:PM], in0=cu[:, 0:PM], scalar=col(3, j), in1=cv[:, 0:PM],
                                                   op0=ALU.mult, op1=ALU.add).then_inc(conv_step, 1)
                        if k == 13:
                            take(u0 + i, s + 2, (6 + 6 * jj) % RING, bs[:, :], M0, NM)
                        if k == 15:
                            take(u0 + i, s + 3, (7 + 6 * jj) % RING, ga[:, :], M0, NM)
                        if k == 17:
                            take(u0 + i, s + 4, (8 + 6 * jj) % RING, go[:, :], M0, NM)
                        if k == 19:
                            take(u0 + i, s + 5, (9 + 6 * jj) % RING, gb[:, :], M0, NM)
                        if (k == 20 and jj == 0) or (k == 19 and jj == 1):
                            v.wait_ge(mixed, j + 1)
                            v.tensor_scalar(mh[:, bass.ds(j, 1), :].rearrange("p a t -> p (a t)"), mx[:, :], 1.0, None,
                                            ALU.mult).then_inc(mix_split, 1)
                            v.wait_ge(mix_split, j * 2 + 1)
                            v.tensor_tensor(ml[:, bass.ds(j, 1), :].rearrange("p a t -> p (a t)"), mx[:, :],
                                            mh[:, bass.ds(j, 1), :].rearrange("p a t -> p (a t)").bitcast(f32),
                                            ALU.subtract).then_inc(mix_split, 1)

            front(0, first=True)
            with v.Fori(0, H - 1) as n:
                back(n)
                front(n + 1)
            back(H - 1)

            def tile_of(t, m, a, b):
                return t[:, bass.ds(m, 1), a:b].rearrange("p a t -> p (a t)")

            v.wait_ge(c_stored, 16 * H)
            v.wait_ge(pc_stored, 16 * H)
            v.sem_inc(x2g_step, 1)
            with v.Fori(0, KT // 4) as n:
                for q in range(4):
                    m = n * 4 + q
                    step(n, 8, U_B, 2 * q)
                    step(n, 8, U_B, 2 * q + 1)
                    v.wait_ge(unit_used, used(n * 8 + (U_B + 2 * q + 1)))
                    v.wait_ge(sq_done, m + 1)
                    v.wait_ge(x2g_step, m * 2 + 1)
                    v.tensor_tensor(x2s[:, :], bank[q][:, 0:NM], tile_of(xres, m, M0, NT), ALU.add).then_inc(evacuated, 1)
                    v.wait_ge(evacuated, out_of(n * 4 + (S_B + q)))
                    v.tensor_scalar(tile_of(xh, m, 0, NM), x2s[:, :], col(1, m), None, ALU.mult).then_inc(x2g_step, 1)
                    v.tensor_scalar(tile_of(xres, m, M0, NT), x2s[:, :], 1.0, None, ALU.mult)
                    v.wait_ge(x2g_step, m * 2 + 2)
                    v.scalar_tensor_tensor(out=tile_of(xl, m, 0, NM), in0=x2s[:, :], scalar=col(1, m),
                                           in1=tile_of(xh, m, 0, NM).bitcast(f32), op0=ALU.mult,
                                           op1=ALU.subtract).then_inc(x2g_step, 1)
            v.wait_ge(r2_spread, 1)
            v.tensor_scalar(rm2[:, :], aux[0][:, 0:NM], 1.0 / D, EPS, ALU.mult, ALU.add).then_inc(r2_step, 1)
            v.wait_ge(r2_root, 1)
            refine(P, slice(0, NM), rt2, rm2, rbc, r2_step, 1)
            v.wait_ge(r2_step, 6)

            for c in range(CH):
                u0 = U_C + c * U_CH
                s0 = S_C + c * S_CH
                with v.Fori(0, FC // 2) as n:
                    for p in range(2):
                        f = n * 2 + (c * FC + p)
                        for z in range(2):
                            fz = f + (FT if z == 0 else 0)
                            q = 2 * p + z
                            cs = n * 20 + (10 * c * FC + 5 * q)
                            step(n, 8, u0, 2 * q)
                            take(n * 8 + (u0 + 2 * q + 1), None, q, zs[:, z, :], 0, NM)
                            v.wait_ge(evacuated, out_of(n * 4 + (s0 + q)))
                            v.tensor_scalar(up_last[:, :, bass.ds(fz, 1)].rearrange("p t a -> p (t a)"),
                                            zs[:, z, NM - NLAST:NM], 1.0, None, ALU.mult).then_inc(fconv_step, 1)
                            wcol = [vecs[:, bass.ds(fz + (6 * KT + t * 2 * FT), 1)] for t in range(CW)]
                            v.tensor_scalar(cz[:, z, :], zs[:, z, 2:NM], wcol[2], None, ALU.mult).then_inc(fconv_step, 1)
                            v.wait_ge(fconv_step, cs + 2)
                            v.scalar_tensor_tensor(out=cz[:, z, 0:SEQ], in0=zs[:, z, 1:1 + SEQ], scalar=wcol[1],
                                                   in1=cz[:, z, 0:SEQ], op0=ALU.mult, op1=ALU.add).then_inc(fconv_step, 1)
                            v.wait_ge(pre_step, 6)
                            v.tensor_tensor(cz[:, z, SEQ:NF], cz[:, z, SEQ:NF],
                                            pre_f[:, bass.ds(fz, 1), :].rearrange("p a b -> p (a b)"), ALU.add)\
                             .then_inc(fconv_step, 1)
                            v.wait_ge(fconv_step, cs + 3)
                            v.scalar_tensor_tensor(out=cz[:, z, 0:SEQ], in0=zs[:, z, 0:SEQ], scalar=wcol[0],
                                                   in1=cz[:, z, 0:SEQ], op0=ALU.mult, op1=ALU.add).then_inc(fconv_step, 1)
                            step(n, 8, u0, 2 * q + 1)
                        v.wait_ge(hid_done, f + 1)
                        fl = n * 2 + p
                        v.tensor_scalar(tile_of(hh, fl, 0, NF), hid[:, :], 1.0, None, ALU.mult).then_inc(hid_split, 1)
                        v.wait_ge(hid_split, f * 2 + 1)
                        v.tensor_tensor(tile_of(hl, fl, 0, NF), hid[:, :], tile_of(hh, fl, 0, NF).bitcast(f32),
                                        ALU.subtract).then_inc(hid_split, 1)
                u1 = u0 + 4 * FC
                s1 = s0 + 2 * FC
                if c == 0:
                    with v.Fori(0, KT // 4) as n:
                        for q in range(4):
                            step(n, 12, u1, 3 * q)
                            step(n, 12, u1, 3 * q + 1)
                            v.wait_ge(unit_used, used(n * 12 + (u1 + 3 * q + 2)))
                            m = n * 4 + q
                            v.tensor_tensor(tile_of(xres, m, NMETA, NT), bank[q][:, 0:NF], tile_of(xres, m, NMETA, NT),
                                            ALU.add).then_inc(evacuated, 1)
                            step(n, 12, u1, 3 * q + 2)
            v.wait_ge(evacuated, out_of(s1 - 1))
            for m in range(KT):
                for i in range(3):
                    if u1 + 3 * m + i + RING < U_END:
                        step(0, 12, u1, 3 * m + i)
                v.wait_ge(unit_used, used(u1 + 3 * m + 2))
                if m >= 2:
                    v.wait_ge(sq_done, KT + m)
                v.tensor_tensor(x3[:, m % 2, :], bank[m % RING][:, 0:NF], xres[:, m, NMETA:NT], ALU.add).then_inc(x3_step, 1)
                v.wait_ge(x3_step, 2 * m + 1)
                if m >= 2:
                    v.wait_ge(y_turned, m - 1)
                v.tensor_scalar(xg3[:, m % 2, :], x3[:, m % 2, :], vecs[:, 2 * KT + m:2 * KT + m + 1], None,
                                ALU.mult).then_inc(x3_step, 1)
            v.wait_ge(ssqf_done, 1)
            v.tensor_scalar(rfm[:, 0:2], aux[3][:, 0:2], 1.0 / D, EPS, ALU.mult, ALU.add).then_inc(rf_step, 1)
            v.tensor_scalar(rfm[0:NS, 2:3], aux[3][0:NS, 2:3], 1.0 / D, EPS, ALU.mult, ALU.add).then_inc(rf_step, 1)
            v.wait_ge(rf_root, 2)
            refine(P, slice(0, 2), rfr, rfm, rf, rf_step, 2)
            refine(NS, slice(2, 3), rfr, rfm, rf, rf_step, 7)
            v.wait_ge(rf_step, 12)
            v.wait_ge(y_copied, 3 * KT // 4)
            v.tensor_scalar(yt[:, 0, :], yt[:, 0, :], rf[:, 0:1], None, ALU.mult).then_inc(y_done, 1)
            v.tensor_scalar(ys[:, :], ys[:, :], rf[0:NS, 2:3], None, ALU.mult).then_inc(y_done, 1)

        @block.tensor
        def _(pe):
            def turn(out, in_, k):
                return pe.transpose(out, in_, ident[0:k, 0:k])

            pe.sem_inc(unit_used, RING)
            pe.wait_ge(const_done, 3)
            pe.wait_ge(params_in, 16 * 5)
            turn(aux[0][:, 0:6 * KT], var_rows[:, :], 6 * KT)
            for t in range(CW):
                c = 6 * KT + t * 2 * FT
                mm = turn(aux[0][:, c:c + 2 * FT], wf_rows[:, t, :], 2 * FT)
            mm.then_inc(params_turned, 1)
            for k in range(KT):
                if k % (KT // 2) == 0:
                    pe.wait_ge(x_in[k // (KT // 2)], 16 * 5)
                if k >= RING:
                    pe.wait_ge(x_copied, k - RING + 1)
                for j in range(3):
                    r = P if j < 2 else TL
                    mm = turn(bank[k % RING][:, j * P:j * P + r], x_tok[0:r, j, k * P:(k + 1) * P], r)
                mm.then_inc(x_turned, 1)
            pe.wait_ge(gw_scaled, 1)
            pe.wait_ge(x_copied, KT)
            for j in range(3):
                r = P if j < 2 else TL
                for k in range(KT):
                    mm = pe.matmul(aux[1][0:r, 16 * j:16 * j + 16], xres[:, k, j * P:j * P + r], gwg[:, k, :],
                                   start=(k == 0), stop=(k == KT - 1))
            mm.then_inc(gz_done, 1)

            def unit(u, slot, b, k0, kk, rh, rl, c0, c1, first, last, waits=()):
                pe.wait_ge(lo_done, u + 1 + RING)
                for k in range(kk):
                    for kw_, sm, value in waits:
                        if kw_ == k:
                            pe.wait_ge(sm, value)
                    w = slice(k * P, (k + 1) * P)
                    for t, (wt, xt) in enumerate(((w_hi, rh), (w_hi, rl), (w_lo, rh))):
                        mm = pe.matmul(bank[b][:, 0:c1 - c0], wt[:, slot, w], xt[:, k0 + k, c0:c1],
                                       start=(first and k == 0 and t == 0), stop=(last and k == kk - 1 and t == 2))
                mm.then_inc(unit_used, 1)

            def strip(s, u, i, b, rh, rl, c0, c1, need=()):
                for h in range(2):
                    waits = [(k - h * KU, sm, x) for k, sm, x in need if k // KU == h]
                    if h == 1:
                        waits.append((2, evacuated, s + 2))
                    unit(u + h, (i + h) % RING, b, h * KU, KU, rh, rl, c0, c1, h == 0, h == 1, waits)

            def tiles_ready(done, per, start, n):
                return [(0, done, start + per * (n // 2)), (n // 2, done, start + per * (n - 2)),
                        (n - 2, done, start + per * (n - 1)), (n - 1, done, start + per * n)]

            def mix_strip(n, s, c0, c1, need=()):
                strip(n * 16 + s, n * HEAD_U + 2 * s, 2 * s, s % RING, xh, xl, c0, c1, need)

            def front(n, first=False):
                for s in range(4):
                    if first and s == 0:
                        mix_strip(n, 0, M0, NT, [(k, xl_done, k + 1) for k in range(KT)])
                        pe.wait_ge(diag_done, 3)
                        for j in range(3):
                            r = P if j < 2 else TL
                            mm = pe.matmul(aux[0][:, j * P:j * P + r], ones[0:r, :], diag[0:r, j, 0:r], start=True, stop=True)
                        mm.then_inc(r_spread, 1)
                        pe.wait_ge(fconv_in, 16)
                        for t in range(8):
                            mm = turn(aux[2 + t // 4][:, (t % 4) * P:(t % 4 + 1) * P], fc_rows[:, t, :], P)
                            if t % 4 == 3:
                                mm.then_inc(f_turned, 1)
                    else:
                        mix_strip(n, s, M0 if s == 0 else 0, NT)
                    if first and s == 1:
                        pe.wait_ge(r_done, 1)
                        for t in range(3):
                            mm = turn(aux[0][:, t * P:(t + 1) * P], fc_rows[:, 8 + t, :], P)
                        mm.then_inc(f_turned, 1)
                        pe.wait_ge(states_in, 48)
                        pe.wait_ge(copied, 3)
                        for t in range(2):
                            turn(aux[2][:, t * P:(t + 1) * P], sc_rows[:, t, :], P)
                        turn(aux[2][:, 2 * P:2 * P + NS * H], n_rows[:, :], NS * H).then_inc(f_turned, 1)
                        pe.wait_ge(g_step, 6)
                        for j in range(3):
                            r = P if j < 2 else TL
                            turn(aux[3][0:H, j * P:j * P + r], lft[0:r, j, :], r)
                            mm = turn(aux[1][0:H, j * P:j * P + r], gz[0:r, j, 0:H], r)
                        mm.then_inc(g_turned, 1)
                    if first and s == 2:
                        pe.wait_ge(s_step, 4)
                        for j in range(3):
                            r = P if j < 2 else T2
                            mm = turn(aux[3][0:r, j * H:(j + 1) * H], aa[:, j * P:j * P + r], H)
                        mm.then_inc(a_turned, 1)

            def back(n):
                for s in range(4, 16):
                    wide = (s - 4) % 6 < 2
                    mix_strip(n, s, C0 if wide else M0, NT)
                    if s == 4:
                        pe.wait_ge(evacuated, out_of(n * 16 + 3))
                        for c0, k0, rows_, q0, nq in ((0, 0, P, 0, PM), (W1, P, P, Q1, PM - Q1), (W2, 2 * P, T2, Q2, T2)):
                            mm = pe.matmul(aux[0][0:rows_, c0:c0 + nq], k_t[:, k0:k0 + rows_], q_t[:, q0:q0 + nq],
                                           start=True, stop=True)
                        mm.then_inc(scores_done, 1)
                        for t in range(2):
                            for w in range(2):
                                turn(aux[1][:, t * DV + w * P:t * DV + (w + 1) * P], v_t[:, w, t * P:(t + 1) * P], P)
                            turn(aux[2][:, t * P:(t + 1) * P], k_t[:, t * P:(t + 1) * P], P)
                        for w in range(2):
                            turn(aux[2][0:T2, (2 + w) * P:(3 + w) * P], v_t[:, w, 2 * P:TP], P)
                            turn(aux[3][0:NS, (1 + w) * P:(2 + w) * P], v_t[:, w, TP:NT], P)
                        turn(aux[3][0:T2, 0:P], k_t[:, 2 * P:TP], P).then_inc(kv_turned, 1)
                    if s == 6:
                        pe.wait_ge(p_done, n + 1)
                        pe.wait_ge(c_in, n * 16 + 16)
                        for b in range(NS):
                            for w in range(2):
                                pe.matmul(aux[0][:, PM + w * NS + b:PM + w * NS + b + 1], c_st[:, b, w * P:(w + 1) * P],
                                          q_t[:, PM + b:PM + b + 1], start=True, stop=True)
                        pe.wait_ge(qk_done, n + 1)
                        pe.wait_ge(qn_done, n + 1)
                        pe.matmul(aux[0][:, PM + 2 * NS:PM + 4 * NS], ones[:, :], qp[:, :], start=True, stop=True)\
                          .then_inc(sample_done, 1)
                        pe.wait_ge(kv_done, n + 1)
                        for a in range(3):
                            for t, (c0, q0) in enumerate(((0, 0), (W1, Q1), (W2, Q2))):
                                lhs = ones[:, :] if a == 2 else v_tok[:, t, a * P:(a + 1) * P]
                                mm = pe.matmul(aux[a][:, q0:PM], lhs, pt[:, c0:c0 + PM - q0], start=(t == 0), stop=(t == 2))
                        mm.then_inc(num_done, 1)
                        for t in range(3):
                            mm = pe.matmul(aux[3][:, 0:DV + 1], kg[:, t, :], v_tok[:, t, :], start=(t == 0), stop=(t == 2))
                        mm.then_inc(cn_done, 1)

            front(0, first=True)
            pe.wait_ge(a3_done, 2)
            pe.wait_ge(copied, 5)
            pe.wait_ge(const_done, 18)
            with pe.Fori(0, H - 1) as n:
                back(n)
                front(n + 1)
            back(H - 1)

            def out_strip(i, q, need=()):
                strip(i * 4 + (S_B + q), i * 8 + (U_B + 2 * q), 2 * q, q, mh, ml, 0, NM, need)

            out_strip(0, 0, tiles_ready(mix_split, 2, 0, KT))
            for q in range(1, 4):
                out_strip(0, q)
            with pe.Fori(1, KT // 4) as i:
                for q in range(4):
                    out_strip(i, q)
            pe.wait_ge(n_step, 2 * H)
            for t in range(NLAST):
                turn(aux[1 + t // 4][0:KT, (t % 4) * P:(t % 4 + 1) * P], cu_last[:, t, :], P)
            turn(aux[3][0:NS * H, 2 * P:3 * P], n_new[:, :, :].rearrange("p b h -> p (b h)"), P)
            turn(aux[3][0:H, 3 * P:4 * P], pn_new[:, :], P).then_inc(last_turned, 1)

            def up_strip(c, i, q, need=()):
                strip(i * 4 + (S_C + c * S_CH + q), i * 8 + (U_C + c * U_CH + 2 * q), 2 * q, q, xh, xl, 0, NM, need)

            def down_strip(c, i, q, need=(), bank_free=None):
                u = i * 12 + (U_C + c * U_CH + 4 * FC + 3 * q)
                for h, (k, kk) in enumerate(DOWN_UNITS):
                    waits = [(x - k, sm, value) for x, sm, value in need if k <= x < k + kk]
                    if h == 2 and bank_free is not None:
                        waits.append((2,) + bank_free)
                    unit(u + h, (3 * q + h) % RING, q, k, kk, hh, hl, 0, NF, h == 0, h == len(DOWN_UNITS) - 1, waits)

            for c in range(CH):
                if c == 0:
                    up_strip(0, 0, 0, tiles_ready(x2g_step, 2, 1, KT))
                    pe.wait_ge(acc_done, KT + 1)
                    pe.matmul(aux[0][:, 0:NM], ones[:, :], acc[:, :], start=True, stop=True).then_inc(r2_spread, 1)
                    for q in range(1, 4):
                        up_strip(0, 0, q)
                with pe.Fori(1 if c == 0 else 0, FC // 2) as i:
                    for q in range(4):
                        up_strip(c, i, q)
                s1 = S_C + c * S_CH + 2 * FC
                hid_need = tiles_ready(hid_split, 2, 2 * c * FC, FC)
                if c == 0:
                    for q in range(4):
                        down_strip(0, 0, q, hid_need if q == 0 else (), (evacuated, s1 + q + 2))
                    with pe.Fori(1, KT // 4) as i:
                        for q in range(4):
                            down_strip(0, i, q, (), (evacuated, i * 4 + (s1 + q + 2)))

            def turn_y(m):
                pe.wait_ge(x3_step, 2 * m + 2)
                if m % 4 == 0:
                    pe.wait_ge(up_copied, 3)
                    pe.wait_ge(y_copied, 3 * (m // 4))
                o = (m % 4) * P
                turn(aux[0][:, o:o + P], xg3[:, m % 2, 0:P], P)
                turn(aux[1][:, o:o + P], xg3[:, m % 2, P:2 * P], P)
                turn(aux[2][0:NS, o:o + P], xg3[:, m % 2, 2 * P:NF], P).then_inc(y_turned, 1)

            for m in range(KT):
                free = (evacuated, s1 + m + 2) if m < RING - 1 else (x3_step, 2 * (m + 1 - RING) + 1)
                down_strip(1, m // 4, m % 4, hid_need if m == 0 else (), free)
                if m == 0:
                    pe.wait_ge(last_copied, 2)
                    for t in range(NLAST):
                        mm = turn(aux[t // 4][0:2 * FT, (t % 4) * P:(t % 4 + 1) * P], up_last[:, t, :], P)
                        if t % 4 == 3 or t == NLAST - 1:
                            mm.then_inc(up_turned, 1)
                else:
                    turn_y(m - 1)
            turn_y(KT - 1)
            pe.wait_ge(acc_done, 2 * KT + 1)
            for j in range(3):
                r = P if j < 2 else NS
                mm = pe.matmul(aux[3][0:r, j:j + 1], acc[:, j * P:j * P + r], ones[:, 0:1], start=True, stop=True)
            mm.then_inc(ssqf_done, 1)


_INS = ['x_prompt', 'x_sample', 'state_mlstm_C', 'state_mlstm_n', 'state_mlstm_m', 'state_shortconv',
        'state_ffnconv', 'meta_tokens', 'norm1_g', 'w_in', 'b_if', 'w_shortconv', 'w_out', 'norm2_g',
        'w_up', 'w_ffconv', 'w_down', 'norm_f_g']


def out_shapes(a):
    depth, nb, heads, dk, dv = a['state_mlstm_C'].shape
    b, seq, d = a['x_prompt'].shape
    rows, ff2 = a['state_ffnconv'].shape[2:]
    return [(b, seq, d), a['x_sample'].shape, (depth, b, heads, dk, dv), (depth, b, heads, dk), (depth, b, heads),
            (depth, b, rows, d), (depth, b, rows, ff2), (depth, nb, heads, dk, dv), (depth, nb, heads, dk),
            (depth, nb, heads), (depth, nb, rows, d), (depth, nb, rows, ff2)]


def kernel(**inputs):
    import concourse.bacc as _bacc
    from concourse import mybir as _mybir
    from concourse.bass_utils import run_bass_kernel_spmd as _run
    f32 = _mybir.dt.float32
    arrays = {n: np.ascontiguousarray(inputs[n]) for n in _INS}
    nc = _bacc.Bacc("TRN2", target_bir_lowering=False, num_devices=1)
    ins = [nc.dram_tensor(f"in_{n}", arrays[n].shape, f32, kind="ExternalInput").ap() for n in _INS]
    outs = [nc.dram_tensor(f"out_{i}", s, f32, kind="ExternalOutput").ap() for i, s in enumerate(out_shapes(arrays))]
    nb, heads, _, dv = arrays['state_mlstm_C'].shape[1:]
    seq_w = arrays['x_prompt'].shape[1] + arrays['w_shortconv'].shape[1] - 1
    rows = nc.dram_tensor("scratch_rows", (heads, 2 * seq_w + 3 * nb), f32, kind="Internal").ap()
    vrows = nc.dram_tensor("scratch_v", (heads, nb * dv), f32, kind="Internal").ap()
    hybrid_decoder_step(nc, ins, outs, rows, vrows)
    r = _run(nc, [{f"in_{n}": arrays[n] for n in _INS}], core_ids=[0])
    return tuple(r.results[0][f"out_{i}"] for i in range(len(outs)))
```

```python
import numpy as np
import concourse.bass as bass
from concourse import mybir
from contextlib import ExitStack


def hybrid_decoder_step(nc, ins, outs, scratch_rows, scratch_v):
    f32, f32r = mybir.dt.float32, mybir.dt.float32r
    ALU, ACT = mybir.AluOpType, mybir.ActivationFunctionType

    (x_prompt, x_sample, state_C, state_n, state_m, state_sconv, state_fconv, meta, norm1_g,
     w_in, b_if, w_sconv, w_out, norm2_g, w_up, w_fconv, w_down, norm_f_g) = ins
    (y_prompt, y_sample, p_C, p_n, p_m, p_sconv, p_fconv,
     s_C, s_n, s_m, s_sconv, s_fconv) = outs

    P = 128
    D = w_in.shape[1]
    NMETA = meta.shape[0]
    SEQ = x_prompt.shape[1]
    NS = x_sample.shape[0]
    H = state_C.shape[2]
    DK, DV = state_C.shape[3], state_C.shape[4]
    DFF = w_down.shape[1]
    EPS = 1e-6
    KSCALE = DK ** -0.5
    KT = D // P
    FT = DFF // P
    TP = NMETA + SEQ
    NT = TP + NS
    CW = w_sconv.shape[1]
    C0 = NMETA - 2 * (CW - 1)
    M0 = NMETA - (CW - 1)
    NCU = NT - C0
    NM = NT - M0
    PM = TP - M0
    NF = NT - NMETA
    T2 = TP - 2 * P
    TL = NT - 2 * P
    NLAST = CW - 1 + NS
    OU, OC, OB = 0, D, 2 * D
    OQ = 3 * D
    OK = OQ + H * DK
    OV = OK + H * DK
    OO = OV + H * DV
    OIF = OO + H * DV
    OGA = OIF + 2 * H
    OGB = OGA + D

    KU = 8
    RING = 4
    HST = 15
    CH = 2
    FC = FT // CH
    DOWN_UNITS = ((0, 8), (8, 8), (16, FC - 16))
    HEAD_U = 32
    U_B = H * HEAD_U
    U_C = U_B + 2 * KT
    U_CH = 4 * FC + 3 * KT
    S_B = U_B // 2
    S_C = S_B + KT
    S_CH = 2 * FC + KT
    U_END = U_C + CH * U_CH
    R_EM, R_DEC, R_W, R_ES, RW = PM, 2 * PM, 2 * PM + NS, 2 * PM + 2 * NS, 2 * PM + 3 * NS
    Q1, Q2 = P - M0, 2 * P - M0
    W1 = PM
    W2 = W1 + PM - Q1
    WG = W2 + T2
    WN = WG + 3
    GF = 32
    GR = GF + H

    ctx = ExitStack()
    with ctx:
        def sb(name, shape, dt=f32):
            return ctx.enter_context(nc.sbuf_tensor(name, shape, dt))

        def sem(name):
            return ctx.enter_context(nc.semaphore(name))

        xres = sb("xres", [P, KT, NT])
        xh = sb("xh", [P, KT, NT], f32r)
        xl = sb("xl", [P, KT, NT], f32r)
        w_raw = sb("w_raw", [P, RING, KU * P])
        w_hi = sb("w_hi", [P, RING, KU * P], f32r)
        w_lo = sb("w_lo", [P, RING, KU * P], f32r)
        ident = sb("ident", [P, P])
        ones = sb("ones", [P, P])
        vecs = sb("vecs", [P, 6 * KT + CW * 2 * FT])
        rbc = sb("rbc", [P, NT])
        pre_s = sb("pre_s", [P, KT, NS])
        pre_f = sb("pre_f", [P, 2 * FT, NS])
        n_new = sb("n_new", [P, NS, H])
        pn_new = sb("pn_new", [P, H])
        cu_last = sb("cu_last", [P, NLAST, KT])
        up_last = sb("up_last", [P, NLAST, 2 * FT])
        acc = sb("acc", [P, NM])
        scn = sb("scn", [P, 2 * P + NS * H])
        a3 = sb("a3", [P, 3, H])
        scale_t = sb("scale_t", [P, NS])

        base = (nc.sbuf_base + 31) // 32 * 32
        REGION = (nc.sbuf_usable_end - base - 64) // 32 * 32
        sb("region", [P, REGION // 4])
        cursor = [0]

        def at(name, shape, dt=f32):
            size = int(np.prod(shape[1:])) * 4
            size = (size + 31) // 32 * 32
            t = nc.alloc_sbuf_tensor_at(name, shape, dt, offset=base + cursor[0])
            cursor[0] += size
            assert cursor[0] <= REGION, (name, cursor[0])
            return t

        mh = at("mh", [P, KT, NM], f32r)
        ml = at("ml", [P, KT, NM], f32r)
        c_st = at("c_st", [P, NS, DV])
        vb = at("vb", [P, NS, DV])
        q_t = at("q_t", [P, NM])
        k_t = at("k_t", [P, NT])
        v_t = at("v_t", [P, 2, NT])
        v_tok = at("v_tok", [P, 3, DV + 1])
        kg = at("kg", [P, 3, DK])
        arg = at("arg", [P, WN])
        wx = at("wx", [P, WN])
        mask = at("mask", [P, WN])
        pt = at("pt", [P, WG])
        rb = at("rb", [P, RW])
        den = at("den", [P, NM])
        rden = at("rden", [P, NM])
        h_t = at("h_t", [P, 2, NM])
        pc = at("pc", [P, DV + 1])
        vs = at("vs", [NS, DV])
        us = at("us", [P, NCU])
        cgs = at("cgs", [P, NCU])
        cu = at("cu", [P, NCU])
        cv = at("cv", [P, NM])
        bs = at("bs", [P, NM])
        ga = at("ga", [P, NM])
        go = at("go", [P, NM])
        gb = at("gb", [P, NM])
        sa = at("sa", [P, NM])
        so = at("so", [P, NM])
        sbm = at("sbm", [P, NM])
        a_gated = at("a_gated", [P, NM])
        mx = at("mx", [P, NM])
        g3 = at("g3", [P, 3])
        wsc = at("wsc", [P, NS])
        kw = at("kw", [P, NS])
        qp = at("qp", [P, 2 * NS])
        sn = at("sn", [P, NS])
        s_s = at("s_s", [P, NS])
        dq = at("dq", [P, NS])
        num_s = at("num_s", [P, 2, NS])
        sv = at("sv", [P, 2, NS])
        cursor[0] = 0
        x_tok = at("x_tok", [P, 3, D])
        var_rows = at("var_rows", [6 * KT, P])
        wf_rows = at("wf_rows", [2 * FT, CW, P])
        sc_rows = at("sc_rows", [P, 2, P])
        n_rows = at("n_rows", [NS * H, P])
        gwh = at("gwh", [P, KT, GR], f32r)
        gwl = at("gwl", [P, KT, GR], f32r)
        b_col = at("b_col", [GR, 1])
        ssq = at("ssq", [P, 3])
        rms = at("rms", [P, 3])
        msq = at("msq", [P, 3])
        rtok = at("rtok", [P, 3])
        assert cursor[0] <= 2 * KT * NM * 4
        cursor[0] = 2 * KT * NM * 4
        fc_rows = at("fc_rows", [P, 11, P])
        fct = at("fct", [P, NS, CW - 1, 2 * FT])
        tmp_f = at("tmp_f", [P, 2 * FT, NS])
        gw = at("gw", [P, KT, 2 * H])
        gex = at("gex", [GR, NT])
        assert cursor[0] <= 2 * KT * NM * 4 + 2 * NS * DV * 4
        cursor[0] = 2 * KT * NM * 4 + 2 * NS * DV * 4 + 22 * 1024
        sq_junk = at("sq_junk", [P, D])
        cursor[0] = 2 * KT * NM * 4 + 2 * NS * DV * 4 + 30 * 1024
        diag = at("diag", [P, 3, P])
        gz = at("gz", [GR, NT])
        gabs = at("gabs", [GR, NT])
        lf = at("lf", [H, NT])
        ig = gz[0:H, :]
        bcum = at("bcum", [H, TP])
        a_row = at("a_row", [H, TP])
        a_max = at("a_max", [H, TP])
        m_row = at("m_row", [H, TP])
        pre_exp = at("pre_exp", [H, PM + 3 * NS])
        rows = at("rows", [H, RW])
        mp = at("mp", [H, NS])
        lf_m = at("lf_m", [H, NS])
        m_samp = at("m_samp", [H, NS])
        ones_row = at("ones_row", [H, TP])
        cursor[0] = 2 * KT * NM * 4
        x2s = at("x2s", [P, NM])
        sqs = at("sqs", [P, NM])
        cursor_co = cursor[0]
        co = at("co", [KT, NLAST, P])
        no = at("no", [NS * H, P])
        pno = at("pno", [H, P])
        rm2 = at("rm2", [P, NM])
        rt2 = at("rt2", [P, NM])
        zs = at("zs", [P, 2, NM])
        cz = at("cz", [P, 2, NF])
        sg = at("sg", [P, NF])
        gg = at("gg", [P, NF])
        hid = at("hid", [P, NF])
        x3 = at("x3", [P, 2, NF])
        xg3 = at("xg3", [P, 2, NF])
        rf = at("rf", [P, 3])
        rfm = at("rfm", [P, 3])
        rfr = at("rfr", [P, 3])
        hh_b = cursor[0]
        cursor[0] = 0
        hl = at("hl", [P, FC, NF], f32r)
        cursor[0] = hh_b
        hh = at("hh", [P, FC, NF], f32r)
        yt = at("yt", [P, 2, D])
        cursor[0] = FC * NF * 4
        ys = at("ys", [NS, D])
        cursor[0] = cursor_co
        uo = at("uo", [2 * FT, NLAST, P])

        bank = [ctx.enter_context(nc.psum_tensor(f"strip{i}", [P, 512], f32)) for i in range(RING)]
        aux = [ctx.enter_context(nc.psum_tensor(f"aux{i}", [P, 512], f32)) for i in range(4)]

        unit_landed = [sem(f"unit_landed{i}") for i in range(RING)]
        hi_done = sem("hi_done")
        lo_done = sem("lo_done")
        unit_used = sem("unit_used")
        evacuated = sem("evacuated")
        params_in, states_in, gates_in = sem("params_in"), sem("states_in"), sem("gates_in")
        x_in = [sem("x_in0"), sem("x_in1")]
        fconv_in = sem("fconv_in")
        const_done = sem("const_done")
        params_turned, copied = sem("params_turned"), sem("copied")
        x_turned, x_copied, xh_done, xl_done = sem("x_turned"), sem("x_copied"), sem("xh_done"), sem("xl_done")
        gw_split, gz_done, scale_done, msq_clear, bias_in = (
            sem("gw_split"), sem("gz_done"), sem("scale_done"), sem("msq_clear"), sem("bias_in"))
        ssq_done, ms_done, rms_done, rtok_done, diag_done = (
            sem("ssq_done"), sem("ms_done"), sem("rms_done"), sem("rtok_done"), sem("diag_done"))
        r_spread, r_done = sem("r_spread"), sem("r_done")
        f_turned, g_step, g_act = sem("f_turned"), sem("g_step"), sem("g_act")
        s_step, a_turned, a3_done = sem("s_step"), sem("a_turned"), sem("a3_done")
        rows_done, rows_stored, rb_in = sem("rows_done"), sem("rows_stored"), sem("rb_in")
        pre_step = sem("pre_step")
        c_in, c_stored, vs_stored, vb_in, pc_stored = (
            sem("c_in"), sem("c_stored"), sem("vs_stored"), sem("vb_in"), sem("pc_stored"))
        arg_done, exp_done, masked, g3_done, p_done = (
            sem("arg_done"), sem("exp_done"), sem("masked"), sem("g3_done"), sem("p_done"))
        scores_done, kv_turned, kv_done, vs_done = (
            sem("scores_done"), sem("kv_turned"), sem("kv_done"), sem("vs_done"))
        wsc_done, kw_done, qk_done, qn_done, sn_done = (
            sem("wsc_done"), sem("kw_done"), sem("qk_done"), sem("qn_done"), sem("sn_done"))
        sample_done, num_done, cn_done, pc_done = (
            sem("sample_done"), sem("num_done"), sem("cn_done"), sem("pc_done"))
        h_step, n_step = sem("h_step"), sem("n_step")
        vk_done, dec_done, c_updated = sem("vk_done"), sem("dec_done"), sem("c_updated")
        cu_done, conv_step, a_done, ag_done, p_gate, b_done, mixed, mix_split = (
            sem("cu_done"), sem("conv_step"), sem("a_done"), sem("ag_done"), sem("p_gate"),
            sem("b_done"), sem("mixed"), sem("mix_split"))
        sig_a, sig_o, sig_b = sem("sig_a"), sem("sig_o"), sem("sig_b")
        sq_done, acc_done, x2g_step, acc_clear = (
            sem("sq_done"), sem("acc_done"), sem("x2g_step"), sem("acc_clear"))
        last_turned, last_copied, r2_spread, r2_step, r2_root = (
            sem("last_turned"), sem("last_copied"), sem("r2_spread"), sem("r2_step"), sem("r2_root"))
        fconv_step, sig_f, gg_done, hid_done, hid_split = (
            sem("fconv_step"), sem("sig_f"), sem("gg_done"), sem("hid_done"), sem("hid_split"))
        x3_step, y_turned, y_copied, ssqf_done, rf_step, rf_root, y_done, y1_done = (
            sem("x3_step"), sem("y_turned"), sem("y_copied"), sem("ssqf_done"), sem("rf_step"),
            sem("rf_root"), sem("y_done"), sem("y1_done"))
        up_turned, up_copied = sem("up_turned"), sem("up_copied")
        last_stored, moved, stored = sem("last_stored"), sem("moved"), sem("stored")

        block = ctx.enter_context(nc.Block())

        def used(u):
            return u + 1 + RING

        def out_of(s):
            return s + 1 + RING

        def col(c, j):
            return vecs[:, bass.ds(c * KT + j, 1)]

        @block.sync
        def _(sp):
            x_t = [(0, 0, NMETA, meta), (0, NMETA, P, x_prompt[0, 0:P - NMETA, :]),
                   (1, 0, P, x_prompt[0, P - NMETA:2 * P - NMETA, :]),
                   (2, 0, T2, x_prompt[0, 2 * P - NMETA:SEQ, :]),
                   (2, T2, TL, x_sample[:, 0, :])]
            for h in range(2):
                for j, a, b, src in x_t:
                    c = slice(h * D // 2, (h + 1) * D // 2)
                    sp.dma_start(x_tok[a:b, j, c], src[:, c]).then_inc(x_in[h], 16)
            sp.sem_inc(lo_done, RING)

            def load(u, slot, src, kk):
                sp.wait_ge(lo_done, u + 1)
                sp.dma_start(w_raw[:, slot, 0:kk * P].rearrange("p (k n) -> p k n", k=kk),
                             src).then_inc(unit_landed[slot], 16)

            w_in_v = w_in[0].rearrange("(k p) n -> p k n", p=P)
            w_out_v = w_out[0].rearrange("(k p) n -> p k n", p=P)
            w_up_v = w_up[0].rearrange("(k p) n -> p k n", p=P)
            w_down_v = w_down[0].rearrange("(k p) n -> p k n", p=P)

            def load_strip(u, i, view, c):
                for h in range(2):
                    load(u + h, (i + h) % RING, view[:, h * KU:(h + 1) * KU, bass.ds(c, P)], KU)

            def front(n):
                for s, c in enumerate((OQ + n * DK, OK + n * DK, OV + n * DV, OV + n * DV + P)):
                    load_strip(n * HEAD_U + 2 * s, 2 * s, w_in_v, c)

            def back(n):
                for jj in range(2):
                    for s, o in enumerate((OU, OC, OB, OGA, OO, OGB)):
                        load_strip(n * HEAD_U + 8 + 12 * jj + 2 * s, 2 * s, w_in_v, n * DV + o + jj * P)

            front(0)
            with sp.Fori(0, H - 1) as n:
                back(n)
                front(n + 1)
            back(H - 1)
            with sp.Fori(0, KT // 4) as i:
                for q in range(4):
                    load_strip(i * 8 + (U_B + 2 * q), 2 * q, w_out_v, i * (4 * P) + q * P)
            for c in range(CH):
                u0 = U_C + c * U_CH
                with sp.Fori(1, FC // 2 + 1) as i:
                    for p in range(2):
                        f = i * (2 * P) + (c * FC + p - 2) * P
                        load_strip(i * 8 + (u0 + 4 * p - 8), 0, w_up_v, f + DFF)
                        load_strip(i * 8 + (u0 + 4 * p - 6), 2, w_up_v, f)
                u1 = u0 + 4 * FC
                with sp.Fori(0, KT // 4) as i:
                    for q in range(4):
                        for h, (k, kk) in enumerate(DOWN_UNITS):
                            load(i * 12 + (u1 + 3 * q + h), (3 * q + h) % RING,
                                 w_down_v[:, c * FC + k:c * FC + k + kk, bass.ds(i * (4 * P) + q * P, P)], kk)
            for h in range(4):
                c = slice(h * D // 4, (h + 1) * D // 4)
                sp.wait_ge(y_done, h + 1)
                sp.dma_start(y_prompt[0, 0:P, c], yt[:, 0, c]).then_inc(stored, 16)
            sp.wait_ge(y_done, 5)
            sp.dma_start(y_sample[:, 0, :], ys[:, :]).then_inc(stored, 16)

        @block.gpsimd
        def _(g):
            g.memset(ident[:, :], 0.0).then_inc(const_done, 1)
            g.memset(ones[:, :], 1.0).then_inc(const_done, 1)
            g.wait_ge(const_done, 2)
            g.affine_select(out=ident[:, :], in_=ident[:, :], compare_op=ALU.not_equal, fill=1.0,
                            base=0, pattern=[[-1, P]], channel_multiplier=1).then_inc(const_done, 1)
            g.memset(acc[:, :], 0.0).then_inc(const_done, 1)
            g.memset(msq[:, :], 1.0).then_inc(msq_clear, 1)
            g.memset(b_col[:, :], 0.0).then_inc(const_done, 1)
            g.memset(a3[:, :, :], 0.0).then_inc(const_done, 1)
            g.memset(ones_row[:, :], 1.0).then_inc(const_done, 1)
            g.memset(gwh[:, :, :].bitcast(f32), 0.0).then_inc(gw_split, 1)
            g.memset(gwl[:, :, :].bitcast(f32), 0.0).then_inc(gw_split, 1)
            g.wait_ge(gates_in, 16)
            g.wait_ge(gw_split, 2)
            for c in (0, 1):
                o = c * GF
                g.tensor_scalar(gwh[:, :, o:o + H], gw[:, :, c * H:(c + 1) * H], 1.0, None, ALU.mult)\
                 .then_inc(gw_split, 1)
            g.wait_ge(gw_split, 4)
            for c in (0, 1):
                o = c * GF
                g.tensor_tensor(gwl[:, :, o:o + H], gw[:, :, c * H:(c + 1) * H], gwh[:, :, o:o + H].bitcast(f32),
                                ALU.subtract).then_inc(gw_split, 1)
            g.wait_ge(x_in[1], 16 * 5)
            g.dma_start(fc_rows[:, :, :], state_fconv[0].rearrange("b t (f p) -> (b t f) p", p=P)
                        .rearrange("(h r) p -> r h p", r=P)).then_inc(fconv_in, 16)
            g.dma_start(sc_rows[:, :, :], state_sconv[0].rearrange("b t (j p) -> (b t j) p", p=P)
                        .rearrange("(h r) p -> r h p", h=2)).then_inc(states_in, 16)
            g.dma_start(n_rows[:, :], state_n[0].rearrange("b h k -> (b h) k")).then_inc(states_in, 16)
            with nc.allow_non_contiguous_dma(reason="64 stabilisers"):
                g.dma_start(mp[:, :], state_m[0].rearrange("b h -> h b")).then_inc(states_in, 16)
            g.dma_start(s_sconv[0, :, 0, :], state_sconv[0, :, 1, :]).then_inc(moved, 16)
            g.dma_start(s_fconv[0, :, 0, :], state_fconv[0, :, 1, :]).then_inc(moved, 16)
            g.wait_ge(gz_done, 1)
            g.wait_ge(scale_done, 1)
            g.memset(mask[:, :], 1.0).then_inc(const_done, 1)
            g.memset(arg[:, :], 0.0).then_inc(const_done, 1)
            g.memset(pt[:, :], 0.0).then_inc(const_done, 1)
            g.memset(v_tok[:, 0:2, :], 1.0).then_inc(const_done, 1)
            g.memset(v_tok[:, 2, :], 0.0).then_inc(const_done, 1)
            g.memset(kg[:, :, :], 0.0).then_inc(const_done, 1)
            g.wait_ge(const_done, 13)
            g.memset(v_tok[0:T2, 2, DV:DV + 1], 1.0).then_inc(const_done, 1)
            for c0, q0, s0, nr, nq in ((0, M0, 0, P, PM), (W1, P, P, P, PM - Q1), (W2, 2 * P, 2 * P, T2, T2)):
                g.affine_select(out=mask[0:nr, c0:c0 + nq], in_=mask[0:nr, c0:c0 + nq], compare_op=ALU.is_ge,
                                fill=0.0, base=q0 - s0, pattern=[[1, nq]], channel_multiplier=-1)\
                 .then_inc(const_done, 1)
            scv = scn[:, 0:2 * P].rearrange("p (b t j) -> p t j b", b=NS, t=CW - 1)
            g.wait_ge(copied, 5)

            def spread(lo, n):
                return vecs[:, lo:lo + n].unsqueeze(2).broadcast_to([P, n, NS])

            ts = tmp_f[:, 0:KT, :]
            g.tensor_tensor(pre_s[:, :, :], scv[:, 0], spread(3 * KT, KT), ALU.mult).then_inc(pre_step, 1)
            g.tensor_tensor(ts, scv[:, 1], spread(4 * KT, KT), ALU.mult).then_inc(pre_step, 1)
            g.wait_ge(pre_step, 2)
            g.tensor_tensor(pre_s[:, :, :], pre_s[:, :, :], ts, ALU.add).then_inc(pre_step, 1)
            fcv = fct[:, :, :, :].rearrange("p b t f -> p t f b")
            g.tensor_tensor(pre_f[:, :, :], fcv[:, 0], spread(6 * KT, 2 * FT), ALU.mult).then_inc(pre_step, 1)
            g.wait_ge(pre_step, 3)
            g.tensor_tensor(tmp_f[:, :, :], fcv[:, 1], spread(6 * KT + 2 * FT, 2 * FT), ALU.mult)\
             .then_inc(pre_step, 1)
            g.wait_ge(pre_step, 5)
            g.tensor_tensor(pre_f[:, :, :], pre_f[:, :, :], tmp_f[:, :, :], ALU.add).then_inc(pre_step, 1)

            dec = rb[:, R_DEC:R_DEC + NS]

            def back(n):
                s0 = n * 16
                j0 = n * 2
                g.wait_ge(rb_in, n * 16 + 16)
                g.tensor_tensor(wsc[:, :], rb[:, R_W:R_W + NS], scale_t[:, :], ALU.mult).then_inc(wsc_done, 1)
                g.wait_ge(evacuated, out_of(s0 + 1))
                g.tensor_tensor(qp[:, 0:NS], q_t[:, PM:NM], k_t[:, TP:NT], ALU.mult).then_inc(qk_done, 1)
                g.wait_ge(wsc_done, n + 1)
                g.tensor_tensor(kw[:, :], k_t[:, TP:NT], wsc[:, :], ALU.mult).then_inc(kw_done, 1)
                g.wait_ge(exp_done, n + 1)
                g.tensor_tensor(g3[:, :], wx[:, WG:WN], scale_t[:, 0:3], ALU.mult).then_inc(g3_done, 1)
                g.tensor_tensor(wx[:, 0:WG], wx[:, 0:WG], mask[:, 0:WG], ALU.mult).then_inc(masked, 1)
                for jj in range(2):
                    j = j0 + jj
                    s = s0 + 4 + 6 * jj
                    g.wait_ge(evacuated, out_of(s + 1))
                    g.tensor_tensor(cu[:, :], us[:, :], cgs[:, :], ALU.mult).then_inc(cu_done, 1)
                    g.wait_ge(evacuated, out_of(s + 2))
                    g.wait_ge(conv_step, j * 5 + 5)
                    g.tensor_tensor(a_gated[:, :], bs[:, :], cv[:, :], ALU.mult).then_inc(a_done, 1)
                    if jj == 0:
                        g.wait_ge(vb_in, n * 16 + 16)
                        g.wait_ge(kw_done, n + 1)
                        g.tensor_tensor(vb[:, :, :], vb[:, :, :], kw[:, :].unsqueeze(2).broadcast_to([P, NS, DV]),
                                        ALU.mult).then_inc(vk_done, 1)
                        g.wait_ge(sample_done, n + 1)
                        g.tensor_tensor(c_st[:, :, :], c_st[:, :, :], dec.unsqueeze(2).broadcast_to([P, NS, DV]),
                                        ALU.mult).then_inc(dec_done, 1)
                        g.wait_ge(vk_done, n + 1)
                        g.wait_ge(dec_done, n + 1)
                        g.tensor_tensor(c_st[:, :, :], c_st[:, :, :], vb[:, :, :], ALU.add).then_inc(c_updated, 1)
                    g.wait_ge(a_done, j + 1)
                    g.wait_ge(sig_a, j + 1)
                    g.tensor_tensor(a_gated[:, :], a_gated[:, :], sa[:, :], ALU.mult).then_inc(ag_done, 1)
                    g.wait_ge(sig_o, j + 1)
                    g.wait_ge(sig_b, j + 1)
                    g.tensor_tensor(so[:, :], so[:, :], sbm[:, :], ALU.mult).then_inc(p_gate, 1)
                    g.wait_ge(p_gate, j + 1)
                    g.wait_ge(h_step, n * HST + HST)
                    g.tensor_tensor(so[:, :], so[:, :], h_t[:, jj, :], ALU.mult).then_inc(b_done, 1)
                    g.wait_ge(ag_done, j + 1)
                    g.wait_ge(b_done, j + 1)
                    g.tensor_tensor(mx[:, :], a_gated[:, :], so[:, :], ALU.add).then_inc(mixed, 1)

            back(0)
            with g.Fori(1, H) as n:
                back(n)
            g.sem_inc(acc_done, 1)
            with g.Fori(0, KT) as m:
                g.wait_ge(sq_done, m + 2)
                g.wait_ge(acc_done, m + 1)
                g.tensor_tensor(acc[:, :], acc[:, :], sqs[:, :], ALU.add).then_inc(acc_done, 1)
            g.wait_ge(r2_spread, 1)
            g.memset(acc[:, :], 0.0).then_inc(acc_clear, 1)
            g.memset(rfm[:, :], 1.0).then_inc(acc_clear, 1)
            with g.Fori(0, FT) as f:
                g.wait_ge(sig_f, f + 1)
                g.tensor_tensor(gg[:, :], sg[:, :], cz[:, 0, :], ALU.mult).then_inc(gg_done, 1)
                g.wait_ge(fconv_step, f * 10 + 10)
                g.wait_ge(gg_done, f + 1)
                g.tensor_tensor(hid[:, :], gg[:, :], cz[:, 1, :], ALU.mult).then_inc(hid_done, 1)
            g.wait_ge(acc_clear, 1)
            with g.Fori(KT, 2 * KT) as m:
                g.wait_ge(sq_done, m + 2)
                g.wait_ge(acc_done, m + 1)
                g.tensor_tensor(acc[:, 0:NF], acc[:, 0:NF], sqs[:, 0:NF], ALU.add).then_inc(acc_done, 1)

        @block.scalar
        def _(act):
            def split_hi(u, slot, n16):
                act.wait_ge(unit_landed[slot], n16)
                act.wait_ge(unit_used, u + 1)
                act.activation(w_hi[:, slot, :], w_raw[:, slot, :], ACT.Copy).then_inc(hi_done, 1)

            def step(n, per, base_u, i):
                u4 = n * per + (base_u + i + RING)
                split_hi(u4, i % RING, n * (16 * per // RING) + 16 * ((base_u + i) // RING + 2))

            for c, src in enumerate((norm1_g[0], norm2_g[0], norm_f_g)):
                act.dma_start(var_rows[c * KT:(c + 1) * KT, :], src.rearrange("(j p) -> j p", p=P))\
                 .then_inc(params_in, 16)
            act.dma_start(var_rows[3 * KT:6 * KT, :], w_sconv[0].rearrange("c (j p) -> (c j) p", p=P))\
             .then_inc(params_in, 16)
            act.dma_start(wf_rows[:, :, :], w_fconv[0].rearrange("c (f p) -> f c p", p=P)).then_inc(params_in, 16)
            act.dma_start(gw[:, :, :], w_in[0].rearrange("(k p) n -> p k n", p=P)[:, :, OIF:OIF + 2 * H])\
             .then_inc(gates_in, 16)
            act.wait_ge(const_done, 5)
            for c in range(2):
                act.dma_start(b_col[c * GF:c * GF + H, :], b_if[0, c * H:(c + 1) * H].rearrange("(h a) -> h a", a=1))\
                   .then_inc(bias_in, 16)
            act.activation(scale_t[:, :], ones[:, 0:NS], ACT.Copy, scale=KSCALE).then_inc(scale_done, 1)
            act.wait_ge(params_turned, 1)
            act.activation(vecs[:, :], aux[0][:, 0:6 * KT + CW * 2 * FT], ACT.Copy).then_inc(copied, 1)
            act.wait_ge(copied, 1)
            for k in range(KT):
                act.wait_ge(x_turned, k + 1)
                act.activation(xres[:, k, :], bank[k % RING][:, 0:NT], ACT.Copy).then_inc(x_copied, 1)
                act.activation(xh[:, k, :], bank[k % RING][:, 0:NT], ACT.Copy, scale=vecs[:, k:k + 1])\
                 .then_inc(xh_done, 1)

            def squares(j):
                r = P if j < 2 else TL
                if j > 0:
                    act.wait_ge(ssq_done, j)
                act.activation(sq_junk[0:r, :], x_tok[0:r, j, :], ACT.Square, accum_out=ssq[0:r, j:j + 1])\
                 .then_inc(ssq_done, 1)

            act.wait_ge(x_in[0], 16 * 5)
            act.wait_ge(x_in[1], 16 * 5)
            for u in range(RING):
                split_hi(u, u, 16)
            for j in range(3):
                squares(j)
            act.wait_ge(ms_done, 2)
            act.activation(rms[:, :], msq[:, :], ACT.Sqrt).then_inc(rms_done, 1)

            def front(n, first=False):
                for i in range(8):
                    step(n, HEAD_U, 0, i)
                    if first and i == 4:
                        act.wait_ge(g_step, 3)
                        act.activation(gex[GF:GR, :], gabs[GF:GR, :], ACT.Exp).then_inc(g_act, 1)
                        act.wait_ge(g_step, 4)
                        act.activation(gabs[GF:GR, :], gex[GF:GR, :], ACT.Ln).then_inc(g_act, 1)
                    if first and i == 1:
                        for t in range(2):
                            act.wait_ge(f_turned, 1 + t)
                            act.activation(fct[:, :, :, :].rearrange("p b t f -> p (b t f)")[:, 512 * t:512 * t + 512],
                                           aux[2 + t][:, :], ACT.Copy).then_inc(copied, 1)
                    if first and i == 1:
                        act.wait_ge(f_turned, 3)
                        act.activation(fct[:, :, :, :].rearrange("p b t f -> p (b t f)")[:, 1024:11 * P],
                                       aux[0][:, 0:3 * P], ACT.Copy).then_inc(copied, 1)
                    if first and i == 3:
                        act.wait_ge(f_turned, 4)
                        act.activation(scn[:, :], aux[2][:, 0:2 * P + NS * H], ACT.Copy).then_inc(copied, 1)
                    if first and i == 6:
                        act.wait_ge(s_step, 12)
                        act.activation(rows[:, R_EM:RW], pre_exp[:, :], ACT.Exp).then_inc(rows_done, 1)
                        act.wait_ge(rows_done, 1)
                        act.dma_start(scratch_rows, rows[:, :]).then_inc(rows_stored, 16)
                        act.dma_start(p_m.rearrange("a b h -> h (a b)"), m_row[:, TP - 1:TP])\
                         .then_inc(rows_stored, 16)
                        with nc.allow_non_contiguous_dma(reason="64 stabilisers"):
                            act.dma_start(s_m[0].rearrange("b h -> h b"), m_samp[:, :]).then_inc(rows_stored, 16)
                    if i == 7:
                        if not first:
                            act.wait_ge(h_step, n * HST)
                            act.wait_ge(n_step, n * 2)
                            act.wait_ge(c_updated, n)
                            act.wait_ge(c_stored, n * 16)
                            act.wait_ge(pc_stored, n * 16)
                        else:
                            act.wait_ge(pre_step, 6)
                            act.wait_ge(rows_stored, 48)
                        act.dma_start(rb[:, :], scratch_rows[bass.ds(n, 1), :].broadcast_to([P, RW]))\
                         .then_inc(rb_in, 16)
                        act.dma_start(c_st[:, :, :], state_C[0].rearrange("b h k v -> h k b v")[n]).then_inc(c_in, 16)

            def back(n):
                j0 = n * 2
                s0 = n * 16
                for i in range(8, HEAD_U):
                    step(n, HEAD_U, 0, i)
                    if i == 8:
                        act.wait_ge(arg_done, n + 1)
                        act.activation(wx[:, :], arg[:, :], ACT.Exp).then_inc(exp_done, 1)
                    if i == 10:
                        act.wait_ge(kv_turned, n + 1)
                        act.wait_ge(g3_done, n + 1)
                        act.activation(vs[:, :], aux[3][0:NS, P:P + DV], ACT.Copy).then_inc(vs_done, 1)
                        act.activation(v_tok[:, 0:2, 0:DV], aux[1][:, :].rearrange("p (j v) -> p j v", j=2), ACT.Copy)
                        for t in range(2):
                            act.activation(kg[:, t, :], aux[2][:, t * P:(t + 1) * P], ACT.Copy, scale=g3[:, t:t + 1])
                        act.activation(v_tok[0:T2, 2, 0:DV], aux[2][0:T2, 2 * P:2 * P + DV], ACT.Copy)
                        act.activation(kg[0:T2, 2, :], aux[3][0:T2, 0:P], ACT.Copy, scale=g3[0:T2, 2:3])\
                         .then_inc(kv_done, 1)
                        act.wait_ge(vs_done, n + 1)
                        act.dma_start(scratch_v[bass.ds(n, 1), :].rearrange("a (b v) -> (a b) v", b=NS), vs[:, :])\
                           .then_inc(vs_stored, 16)
                    if i == 11:
                        act.wait_ge(vs_stored, n * 16 + 16)
                        act.dma_start(vb[:, :, :].rearrange("p b v -> p (b v)"),
                                      scratch_v[bass.ds(n, 1), :].broadcast_to([P, NS * DV])).then_inc(vb_in, 16)
                    if i == 14:
                        act.wait_ge(cn_done, n + 1)
                        act.activation(pc[:, :], aux[3][:, 0:DV + 1], ACT.Copy).then_inc(pc_done, 1)
                        act.wait_ge(pc_done, n + 1)
                        act.dma_start(p_C[0, 0].rearrange("h k v -> h k v")[n], pc[:, 0:DV]).then_inc(pc_stored, 16)
                    for jj in range(2):
                        if i == 15 + 12 * jj:
                            act.wait_ge(evacuated, out_of(s0 + 7 + 6 * jj))
                            act.activation(sa[:, :], ga[:, :], ACT.Sigmoid).then_inc(sig_a, 1)
                        if i == 17 + 12 * jj:
                            act.wait_ge(evacuated, out_of(s0 + 8 + 6 * jj))
                            act.activation(so[:, :], go[:, :], ACT.Sigmoid).then_inc(sig_o, 1)
                        if i == 19 + 12 * jj:
                            act.wait_ge(evacuated, out_of(s0 + 9 + 6 * jj))
                            act.activation(sbm[:, :], gb[:, :], ACT.Sigmoid).then_inc(sig_b, 1)
                    if i == 24:
                        act.wait_ge(c_updated, n + 1)
                        act.dma_start(s_C[0].rearrange("b h k v -> h k b v")[n], c_st[:, :, :]).then_inc(c_stored, 16)

            front(0, first=True)
            with act.Fori(0, H - 1) as n:
                back(n)
                front(n + 1)
            back(H - 1)

            def square_into(m, src):
                act.wait_ge(acc_done, m + 1)
                act.activation(sqs[:, 0:src.shape[1]], src, ACT.Square).then_inc(sq_done, 1)

            act.sem_inc(sq_done, 1)
            with act.Fori(0, KT // 4) as n:
                for q in range(4):
                    step(n, 8, U_B, 2 * q)
                    step(n, 8, U_B, 2 * q + 1)
                    act.wait_ge(evacuated, out_of(n * 4 + (S_B + q)))
                    square_into(n * 4 + q, x2s[:, :])
            act.wait_ge(last_turned, 1)
            for t in range(2):
                act.activation(co[:, 4 * t:4 * t + 4, :].rearrange("j t p -> j (t p)"), aux[1 + t][0:KT, :], ACT.Copy)
            act.activation(co[:, 8:10, :].rearrange("j t p -> j (t p)"), aux[3][0:KT, 0:2 * P], ACT.Copy)\
             .then_inc(last_copied, 1)
            act.activation(no[:, :], aux[3][0:NS * H, 2 * P:3 * P], ACT.Copy)
            act.activation(pno[:, :], aux[3][0:H, 3 * P:4 * P], ACT.Copy).then_inc(last_copied, 1)
            act.wait_ge(r2_step, 1)
            act.activation(rt2[:, :], rm2[:, :], ACT.Sqrt).then_inc(r2_root, 1)
            act.wait_ge(last_copied, 2)
            act.dma_start(p_sconv[0, 0].rearrange("t (j p) -> j t p", p=P), co[:, 0:CW - 1, :])\
             .then_inc(last_stored, 16)
            act.dma_start(s_sconv[0, :, CW - 2, :].rearrange("b (j p) -> j b p", p=P), co[:, CW - 1:, :])\
             .then_inc(last_stored, 16)
            act.dma_start(s_n[0].rearrange("b h k -> (b h) k"), no[:, :]).then_inc(last_stored, 16)
            act.dma_start(p_n[0, 0], pno[:, :]).then_inc(last_stored, 16)

            for c in range(CH):
                u0 = U_C + c * U_CH
                with act.Fori(0, FC // 2) as n:
                    for p in range(2):
                        step(n, 8, u0, 4 * p)
                        step(n, 8, u0, 4 * p + 1)
                        step(n, 8, u0, 4 * p + 2)
                        act.wait_ge(fconv_step, n * 20 + (10 * c * FC + 10 * p + 5))
                        act.activation(sg[:, :], cz[:, 0, :], ACT.Sigmoid).then_inc(sig_f, 1)
                        step(n, 8, u0, 4 * p + 3)
                u1 = u0 + 4 * FC
                if c == 0:
                    with act.Fori(0, KT // 4) as n:
                        for i in range(12):
                            step(n, 12, u1, i)
            for m in range(KT):
                for i in range(3):
                    if u1 + 3 * m + i + RING < U_END:
                        step(0, 12, u1, 3 * m + i)
                if m == 0:
                    act.wait_ge(last_stored, 16 * 4)
                    for t in range(3):
                        act.wait_ge(up_turned, t + 1)
                        w = min(4, NLAST - 4 * t)
                        act.activation(uo[:, 4 * t:4 * t + w, :].rearrange("f t p -> f (t p)"),
                                       aux[t][0:2 * FT, 0:w * P], ACT.Copy).then_inc(up_copied, 1)
                    act.wait_ge(up_copied, 3)
                    act.dma_start(p_fconv[0, 0].rearrange("t (f p) -> f t p", p=P), uo[:, 0:CW - 1, :])\
                     .then_inc(stored, 16)
                    act.dma_start(s_fconv[0, :, CW - 2, :].rearrange("b (f p) -> f b p", p=P), uo[:, CW - 1:, :])\
                       .then_inc(stored, 16)
                act.wait_ge(x3_step, 2 * m + 1)
                square_into(KT + m, x3[:, m % 2, :])
                if m % 4 == 0 and m > 0:
                    gq = m // 4 - 1
                    act.wait_ge(y_turned, 4 * (gq + 1))
                    for t in range(2):
                        act.activation(yt[:, t, 512 * gq:512 * gq + 512], aux[t][:, :], ACT.Copy)\
                         .then_inc(y_copied, 1)
                    act.activation(ys[:, 512 * gq:512 * gq + 512], aux[2][0:NS, :], ACT.Copy).then_inc(y_copied, 1)
            act.wait_ge(rf_step, 2)
            act.activation(rfr[:, :], rfm[:, :], ACT.Sqrt).then_inc(rf_root, 1)
            act.wait_ge(rf_step, 7)
            act.wait_ge(y_copied, 3 * (KT // 4 - 1))
            act.wait_ge(y_turned, KT)
            for h in range(4):
                c = slice(h * D // 4, (h + 1) * D // 4)
                src = yt[:, 1, c] if h < 3 else aux[1][:, :]
                act.activation(yt[:, 1, c], src, ACT.Copy, scale=rf[:, 1:2]).then_inc(y1_done, 1)
                act.wait_ge(y1_done, h + 1)
                act.dma_start(y_prompt[0, P:2 * P, c], yt[:, 1, c]).then_inc(stored, 16)
            act.wait_ge(pc_stored, 16 * H)
            act.wait_ge(c_stored, 16 * H)
            act.wait_ge(moved, 16 * 2)
            act.wait_ge(stored, 16 * (2 + 4 + 4 + 1))

        @block.vector
        def _(v):
            def split_lo(u, slot):
                v.wait_ge(hi_done, u + 1)
                v.tensor_tensor(w_lo[:, slot, :], w_raw[:, slot, :], w_hi[:, slot, :].bitcast(f32),
                                ALU.subtract).then_inc(lo_done, 1)

            def step(n, per, base_u, i):
                split_lo(n * per + (base_u + i + RING), i % RING)

            def take(u, b, out, c0, width):
                v.wait_ge(unit_used, used(u))
                v.tensor_tensor(out, bank[b][:, 0:width], rbc[:, c0:c0 + width], ALU.mult).then_inc(evacuated, 1)

            def refine(r, c, root, mean, out, done, d0):
                v.reciprocal(out[0:r, c], root[0:r, c]).then_inc(done, 1)
                v.wait_ge(done, d0 + 1)
                v.tensor_tensor(root[0:r, c], out[0:r, c], out[0:r, c], ALU.mult).then_inc(done, 1)
                v.wait_ge(done, d0 + 2)
                v.scalar_tensor_tensor(out=root[0:r, c], in0=root[0:r, c], scalar=-0.5, in1=mean[0:r, c],
                                       op0=ALU.mult, op1=ALU.mult).then_inc(done, 1)
                v.wait_ge(done, d0 + 3)
                v.tensor_scalar(root[0:r, c], root[0:r, c], 1.5, None, ALU.add).then_inc(done, 1)
                v.wait_ge(done, d0 + 4)
                v.tensor_tensor(out[0:r, c], out[0:r, c], root[0:r, c], ALU.mult).then_inc(done, 1)

            v.sem_inc(evacuated, RING)
            for k in range(KT):
                v.wait_ge(xh_done, k + 1)
                v.scalar_tensor_tensor(out=xl[:, k, :], in0=xres[:, k, :], scalar=vecs[:, k:k + 1],
                                       in1=xh[:, k, :].bitcast(f32), op0=ALU.mult, op1=ALU.subtract)\
                                        .then_inc(xl_done, 1)
            for u in range(RING):
                split_lo(u, u)
            v.wait_ge(ssq_done, 3)
            v.wait_ge(msq_clear, 1)
            v.tensor_scalar(msq[:, 0:2], ssq[:, 0:2], 1.0 / D, EPS, ALU.mult, ALU.add).then_inc(ms_done, 1)
            v.tensor_scalar(msq[0:TL, 2:3], ssq[0:TL, 2:3], 1.0 / D, EPS, ALU.mult, ALU.add).then_inc(ms_done, 1)
            v.wait_ge(rms_done, 1)
            refine(P, slice(0, 3), rms, msq, rtok, rtok_done, 0)
            v.wait_ge(rtok_done, 5)
            for j in range(3):
                r = P if j < 2 else TL
                v.tensor_scalar(diag[0:r, j, :], ident[0:r, :], rtok[0:r, j:j + 1], None, ALU.mult)\
                 .then_inc(diag_done, 1)

            def front(n, first=False):
                u0 = n * HEAD_U
                s0 = n * 16
                for i in range(8):
                    step(n, HEAD_U, 0, i)
                    if first and i == 3:
                        v.wait_ge(r_spread, 1)
                        v.tensor_copy(rbc[:, :], aux[3][:, 0:NT]).then_inc(r_done, 1)
                        v.wait_ge(r_done, 1)
                        v.wait_ge(gz_done, 1)
                        v.tensor_tensor(gz[:, :], aux[1][0:GR, 0:NT], rbc[0:GR, :], ALU.mult).then_inc(g_step, 1)
                        v.wait_ge(bias_in, 32)
                        v.wait_ge(g_step, 1)
                        v.tensor_scalar(gz[:, :], gz[:, :], b_col[:, :], None, ALU.add).then_inc(g_step, 1)
                        v.wait_ge(g_step, 2)
                        v.scalar_tensor_tensor(out=gabs[GF:GR, :], in0=gz[GF:GR, :], scalar=-1.0, in1=gz[GF:GR, :],
                                               op0=ALU.mult, op1=ALU.min).then_inc(g_step, 1)
                        take(u0 + 1, 0, q_t[:, :], M0, NM)
                    if first and i == 4:
                        v.wait_ge(g_act, 1)
                        v.tensor_scalar(gex[GF:GR, :], gex[GF:GR, :], 1.0, None, ALU.add).then_inc(g_step, 1)
                        v.wait_ge(g_act, 2)
                        v.scalar_tensor_tensor(out=lf[:, :], in0=gz[GF:GR, :], scalar=0.0, in1=gabs[GF:GR, :],
                                               op0=ALU.min, op1=ALU.subtract).then_inc(s_step, 1)
                        v.wait_ge(s_step, 1)
                        v.tensor_tensor_scan(bcum[:, :], ones_row[:, :], lf[:, 0:TP], 0.0, ALU.mult, ALU.add)\
                         .then_inc(s_step, 1)
                        v.wait_ge(s_step, 2)
                        v.tensor_tensor(a_row[:, :], ig[:, 0:TP], bcum[:, :], ALU.subtract).then_inc(s_step, 1)
                        v.wait_ge(s_step, 3)
                        v.tensor_tensor_scan(a_max[:, :], ones_row[:, :], a_row[:, :], 0.0, ALU.mult, ALU.max)\
                         .then_inc(s_step, 1)
                        v.wait_ge(states_in, 48)
                        v.tensor_tensor(lf_m[:, :], lf[:, TP:NT], mp[:, :], ALU.add).then_inc(s_step, 1)
                        v.wait_ge(s_step, 5)
                        v.tensor_scalar(rows[:, 0:PM], a_max[:, M0:TP], -1.0, None, ALU.mult).then_inc(s_step, 1)
                        v.tensor_tensor(m_row[:, :], bcum[:, :], a_max[:, :], ALU.add).then_inc(s_step, 1)
                        v.tensor_tensor(m_samp[:, :], lf_m[:, :], ig[:, TP:NT], ALU.max).then_inc(s_step, 1)
                        v.wait_ge(s_step, 8)
                        v.tensor_scalar(pre_exp[:, 0:PM], m_row[:, M0:TP], -1.0, None, ALU.mult).then_inc(s_step, 1)
                        v.tensor_tensor(pre_exp[:, PM:PM + NS], lf_m[:, :], m_samp[:, :], ALU.subtract)\
                         .then_inc(s_step, 1)
                        v.tensor_tensor(pre_exp[:, PM + NS:PM + 2 * NS], ig[:, TP:NT], m_samp[:, :], ALU.subtract)\
                         .then_inc(s_step, 1)
                        v.tensor_scalar(pre_exp[:, PM + 2 * NS:PM + 3 * NS], m_samp[:, :], -1.0, None, ALU.mult)\
                         .then_inc(s_step, 1)
                    if i == 1 and not first:
                        take(u0 + 1, 0, q_t[:, :], M0, NM)
                    if i == 3:
                        take(u0 + 3, 1, k_t[:, :], 0, NT)
                    if i == 5:
                        take(u0 + 5, 2, v_t[:, 0, :], 0, NT)
                    if first and i == 7:
                        v.wait_ge(a_turned, 1)
                        v.tensor_copy(a3[:, 0:2, :], aux[3][:, 0:2 * H].rearrange("p (j h) -> p j h", j=2))\
                         .then_inc(a3_done, 1)
                        v.tensor_copy(a3[0:T2, 2, :], aux[3][0:T2, 2 * H:3 * H]).then_inc(a3_done, 1)
                        v.wait_ge(a3_done, 2)
                    if i == 7:
                        take(u0 + 7, 3, v_t[:, 1, :], 0, NT)

            dec = rb[:, R_DEC:R_DEC + NS]

            def back(n):
                u0 = n * HEAD_U
                s0 = n * 16
                hs = n * HST
                last = {9: (us, C0, NCU), 11: (cgs, C0, NCU), 13: (bs, M0, NM), 15: (ga, M0, NM), 17: (go, M0, NM),
                        19: (gb, M0, NM)}
                for i in range(8, HEAD_U):
                    k = 8 + (i - 8) % 12
                    if k in last:
                        out, c0, width = last[k]
                        take(u0 + i, i // 2 % RING, out[:, :], c0, width)
                    step(n, HEAD_U, 0, i)
                    if i == 8:
                        v.wait_ge(rb_in, n * 16 + 16)
                        for j, (c0, q0, nr, nq) in enumerate(((0, 0, P, PM), (W1, Q1, P, PM - Q1), (W2, Q2, T2, T2))):
                            v.tensor_scalar(arg[0:nr, c0:c0 + nq], rb[0:nr, q0:q0 + nq],
                                            a3[0:nr, j, bass.ds(n, 1)], 0.0, ALU.add, ALU.min)
                        v.tensor_scalar(arg[:, WG:WN], a3[:, :, bass.ds(n, 1)].rearrange("p j a -> p (j a)"),
                                        rb[:, PM - 1:PM], 0.0, ALU.add, ALU.min).then_inc(arg_done, 1)
                        v.tensor_scalar(sn[:, :], scn[:, 2 * P:].rearrange("p (b h) -> p b h", b=NS)[:, :, bass.ds(n, 1)]
                                        .rearrange("p b a -> p (b a)"), 1.0, None, ALU.mult).then_inc(sn_done, 1)
                        v.wait_ge(sn_done, n + 1)
                        v.tensor_tensor(qp[:, NS:2 * NS], q_t[:, PM:NM], sn[:, :], ALU.mult).then_inc(qn_done, 1)
                    if i == 10:
                        v.wait_ge(scores_done, n + 1)
                        v.wait_ge(masked, n + 1)
                        v.scalar_tensor_tensor(out=pt[:, 0:W2], in0=aux[0][:, 0:W2], scalar=KSCALE, in1=wx[:, 0:W2],
                                               op0=ALU.mult, op1=ALU.mult)
                        v.scalar_tensor_tensor(out=pt[0:T2, W2:WG], in0=aux[0][0:T2, W2:WG], scalar=KSCALE,
                                               in1=wx[0:T2, W2:WG], op0=ALU.mult, op1=ALU.mult).then_inc(p_done, 1)
                    if i == 14:
                        v.wait_ge(num_done, n + 1)
                        v.tensor_tensor(den[:, 0:PM], aux[2][:, 0:PM], rb[:, R_EM:R_EM + PM], ALU.max)\
                         .then_inc(h_step, 1)
                        v.wait_ge(wsc_done, n + 1)
                        v.tensor_tensor(s_s[:, :], aux[0][:, PM + 2 * NS:PM + 3 * NS], wsc[:, :], ALU.mult)\
                         .then_inc(h_step, 1)
                        v.tensor_tensor(dq[:, :], aux[0][:, PM + 3 * NS:PM + 4 * NS], dec, ALU.mult)\
                         .then_inc(h_step, 1)
                        v.tensor_tensor(num_s[:, :, :], aux[0][:, PM:PM + 2 * NS].rearrange("p (a b) -> p a b", a=2),
                                        dec.unsqueeze(1).broadcast_to([P, 2, NS]), ALU.mult)\
                                         .then_inc(h_step, 1)
                        v.wait_ge(h_step, hs + 1)
                        v.scalar_tensor_tensor(out=den[:, 0:PM], in0=aux[2][:, 0:PM], scalar=-1.0, in1=den[:, 0:PM],
                                               op0=ALU.mult, op1=ALU.max)\
                                                .then_inc(h_step, 1)
                        v.wait_ge(h_step, hs + 3)
                        v.tensor_tensor(dq[:, :], dq[:, :], s_s[:, :], ALU.add)\
                         .then_inc(h_step, 1)
                        v.tensor_tensor(sv[:, :, :], v_t[:, :, TP:NT], s_s[:, :].unsqueeze(1).broadcast_to([P, 2, NS]),
                                        ALU.mult)\
                                         .then_inc(h_step, 1)
                        v.wait_ge(h_step, hs + 6)
                        v.tensor_tensor(den[:, PM:NM], dq[:, :], rb[:, R_ES:R_ES + NS], ALU.max)\
                         .then_inc(h_step, 1)
                        v.wait_ge(h_step, hs + 8)
                        v.scalar_tensor_tensor(out=den[:, PM:NM], in0=dq[:, :], scalar=-1.0, in1=den[:, PM:NM],
                                               op0=ALU.mult, op1=ALU.max)\
                                                .then_inc(h_step, 1)
                        v.tensor_tensor(num_s[:, :, :], num_s[:, :, :], sv[:, :, :], ALU.add)\
                         .then_inc(h_step, 1)
                        v.wait_ge(h_step, hs + 9)
                        v.reciprocal(rden[:, :], den[:, :])\
                         .then_inc(h_step, 1)
                        v.wait_ge(h_step, hs + 11)
                        v.tensor_tensor(h_t[:, :, PM:NM], num_s[:, :, :], rden[:, PM:NM].unsqueeze(1).broadcast_to([P, 2, NS]),
                                        ALU.mult)\
                                         .then_inc(h_step, 1)
                        v.tensor_tensor(h_t[:, 0, 0:PM], aux[0][:, 0:PM], rden[:, 0:PM], ALU.mult)\
                         .then_inc(h_step, 1)
                        v.tensor_tensor(h_t[:, 1, 0:PM], aux[1][:, 0:PM], rden[:, 0:PM], ALU.mult)\
                         .then_inc(h_step, 1)
                        v.tensor_tensor(sn[:, :], sn[:, :], dec, ALU.mult)\
                         .then_inc(h_step, 1)
                    if i == 16:
                        v.wait_ge(h_step, hs + HST)
                        v.wait_ge(kw_done, n + 1)
                        v.tensor_tensor(n_new[:, :, bass.ds(n, 1)].rearrange("p b a -> p (b a)"), sn[:, :], kw[:, :],
                                        ALU.add).then_inc(n_step, 1)
                        v.wait_ge(pc_done, n + 1)
                        v.tensor_scalar(pn_new[:, bass.ds(n, 1)], pc[:, DV:DV + 1], 1.0, None, ALU.mult)\
                         .then_inc(n_step, 1)
                    for jj in range(2):
                        j = n * 2 + jj
                        k = i - 12 * jj
                        if k == 12:
                            v.wait_ge(cu_done, j + 1)
                            v.tensor_scalar(cu_last[:, :, bass.ds(j, 1)].rearrange("p t a -> p (t a)"), cu[:, NCU - NLAST:NCU],
                                            1.0, None, ALU.mult).then_inc(conv_step, 1)
                            v.tensor_scalar(cv[:, :], cu[:, 2:NCU], col(5, j), None, ALU.mult).then_inc(conv_step, 1)
                            v.wait_ge(conv_step, j * 5 + 2)
                            v.scalar_tensor_tensor(out=cv[:, 0:PM], in0=cu[:, 1:1 + PM], scalar=col(4, j), in1=cv[:, 0:PM],
                                                   op0=ALU.mult, op1=ALU.add).then_inc(conv_step, 1)
                            v.wait_ge(pre_step, 3)
                            v.tensor_tensor(cv[:, PM:NM], cv[:, PM:NM], pre_s[:, bass.ds(j, 1), :].rearrange("p a b -> p (a b)"),
                                            ALU.add).then_inc(conv_step, 1)
                            v.wait_ge(conv_step, j * 5 + 3)
                            v.scalar_tensor_tensor(out=cv[:, 0:PM], in0=cu[:, 0:PM], scalar=col(3, j), in1=cv[:, 0:PM],
                                                   op0=ALU.mult, op1=ALU.add).then_inc(conv_step, 1)
                        if (k == 20 and jj == 0) or (k == 19 and jj == 1):
                            v.wait_ge(mixed, j + 1)
                            v.tensor_scalar(mh[:, bass.ds(j, 1), :].rearrange("p a t -> p (a t)"), mx[:, :], 1.0, None,
                                            ALU.mult).then_inc(mix_split, 1)
                            v.wait_ge(mix_split, j * 2 + 1)
                            v.tensor_tensor(ml[:, bass.ds(j, 1), :].rearrange("p a t -> p (a t)"), mx[:, :],
                                            mh[:, bass.ds(j, 1), :].rearrange("p a t -> p (a t)").bitcast(f32),
                                            ALU.subtract).then_inc(mix_split, 1)

            front(0, first=True)
            with v.Fori(0, H - 1) as n:
                back(n)
                front(n + 1)
            back(H - 1)

            def tile_of(t, m, a, b):
                return t[:, bass.ds(m, 1), a:b].rearrange("p a t -> p (a t)")

            v.wait_ge(c_stored, 16 * H)
            v.wait_ge(pc_stored, 16 * H)
            v.sem_inc(x2g_step, 1)
            with v.Fori(0, KT // 4) as n:
                for q in range(4):
                    m = n * 4 + q
                    step(n, 8, U_B, 2 * q)
                    v.wait_ge(unit_used, used(n * 8 + (U_B + 2 * q + 1)))
                    v.wait_ge(sq_done, m + 1)
                    v.wait_ge(x2g_step, m * 2 + 1)
                    v.tensor_tensor(x2s[:, :], bank[q][:, 0:NM], tile_of(xres, m, M0, NT), ALU.add)\
                     .then_inc(evacuated, 1)
                    v.wait_ge(evacuated, out_of(n * 4 + (S_B + q)))
                    v.tensor_scalar(tile_of(xh, m, 0, NM), x2s[:, :], col(1, m), None, ALU.mult).then_inc(x2g_step, 1)
                    v.tensor_scalar(tile_of(xres, m, M0, NT), x2s[:, :], 1.0, None, ALU.mult)
                    v.wait_ge(x2g_step, m * 2 + 2)
                    v.scalar_tensor_tensor(out=tile_of(xl, m, 0, NM), in0=x2s[:, :], scalar=col(1, m),
                                           in1=tile_of(xh, m, 0, NM).bitcast(f32), op0=ALU.mult,
                                           op1=ALU.subtract).then_inc(x2g_step, 1)
                    step(n, 8, U_B, 2 * q + 1)
            v.wait_ge(r2_spread, 1)
            v.tensor_scalar(rm2[:, :], aux[0][:, 0:NM], 1.0 / D, EPS, ALU.mult, ALU.add).then_inc(r2_step, 1)
            v.wait_ge(r2_root, 1)
            refine(P, slice(0, NM), rt2, rm2, rbc, r2_step, 1)
            v.wait_ge(r2_step, 6)

            for c in range(CH):
                u0 = U_C + c * U_CH
                s0 = S_C + c * S_CH
                with v.Fori(0, FC // 2) as n:
                    for p in range(2):
                        f = n * 2 + (c * FC + p)
                        for z in range(2):
                            fz = f + (FT if z == 0 else 0)
                            q = 2 * p + z
                            cs = n * 20 + (10 * c * FC + 5 * q)
                            step(n, 8, u0, 2 * q)
                            take(n * 8 + (u0 + 2 * q + 1), q, zs[:, z, :], 0, NM)
                            v.wait_ge(evacuated, out_of(n * 4 + (s0 + q)))
                            v.tensor_scalar(up_last[:, :, bass.ds(fz, 1)].rearrange("p t a -> p (t a)"),
                                            zs[:, z, NM - NLAST:NM], 1.0, None, ALU.mult).then_inc(fconv_step, 1)
                            wcol = [vecs[:, bass.ds(fz + (6 * KT + t * 2 * FT), 1)] for t in range(CW)]
                            v.tensor_scalar(cz[:, z, :], zs[:, z, 2:NM], wcol[2], None, ALU.mult)\
                             .then_inc(fconv_step, 1)
                            v.wait_ge(fconv_step, cs + 2)
                            v.scalar_tensor_tensor(out=cz[:, z, 0:SEQ], in0=zs[:, z, 1:1 + SEQ], scalar=wcol[1],
                                                   in1=cz[:, z, 0:SEQ], op0=ALU.mult, op1=ALU.add)\
                                                    .then_inc(fconv_step, 1)
                            v.wait_ge(pre_step, 6)
                            v.tensor_tensor(cz[:, z, SEQ:NF], cz[:, z, SEQ:NF],
                                            pre_f[:, bass.ds(fz, 1), :].rearrange("p a b -> p (a b)"), ALU.add)\
                             .then_inc(fconv_step, 1)
                            v.wait_ge(fconv_step, cs + 3)
                            v.scalar_tensor_tensor(out=cz[:, z, 0:SEQ], in0=zs[:, z, 0:SEQ], scalar=wcol[0],
                                                   in1=cz[:, z, 0:SEQ], op0=ALU.mult, op1=ALU.add)\
                                                    .then_inc(fconv_step, 1)
                            step(n, 8, u0, 2 * q + 1)
                        v.wait_ge(hid_done, f + 1)
                        fl = n * 2 + p
                        v.tensor_scalar(tile_of(hh, fl, 0, NF), hid[:, :], 1.0, None, ALU.mult).then_inc(hid_split, 1)
                        v.wait_ge(hid_split, f * 2 + 1)
                        v.tensor_tensor(tile_of(hl, fl, 0, NF), hid[:, :], tile_of(hh, fl, 0, NF).bitcast(f32),
                                        ALU.subtract).then_inc(hid_split, 1)
                u1 = u0 + 4 * FC
                s1 = s0 + 2 * FC
                if c == 0:
                    with v.Fori(0, KT // 4) as n:
                        for q in range(4):
                            step(n, 12, u1, 3 * q)
                            step(n, 12, u1, 3 * q + 1)
                            v.wait_ge(unit_used, used(n * 12 + (u1 + 3 * q + 2)))
                            m = n * 4 + q
                            v.tensor_tensor(tile_of(xres, m, NMETA, NT), bank[q][:, 0:NF], tile_of(xres, m, NMETA, NT),
                                            ALU.add).then_inc(evacuated, 1)
                            step(n, 12, u1, 3 * q + 2)
            v.wait_ge(evacuated, out_of(s1 - 1))
            for m in range(KT):
                for i in range(3):
                    if u1 + 3 * m + i + RING < U_END:
                        step(0, 12, u1, 3 * m + i)
                v.wait_ge(unit_used, used(u1 + 3 * m + 2))
                if m >= 2:
                    v.wait_ge(sq_done, KT + m)
                v.tensor_tensor(x3[:, m % 2, :], bank[m % RING][:, 0:NF], xres[:, m, NMETA:NT], ALU.add)\
                 .then_inc(x3_step, 1)
                v.wait_ge(x3_step, 2 * m + 1)
                if m >= 2:
                    v.wait_ge(y_turned, m - 1)
                v.tensor_scalar(xg3[:, m % 2, :], x3[:, m % 2, :], vecs[:, 2 * KT + m:2 * KT + m + 1], None,
                                ALU.mult).then_inc(x3_step, 1)
            v.wait_ge(ssqf_done, 1)
            v.wait_ge(acc_clear, 2)
            v.tensor_scalar(rfm[:, 0:2], aux[3][:, 0:2], 1.0 / D, EPS, ALU.mult, ALU.add).then_inc(rf_step, 1)
            v.tensor_scalar(rfm[0:NS, 2:3], aux[3][0:NS, 2:3], 1.0 / D, EPS, ALU.mult, ALU.add).then_inc(rf_step, 1)
            v.wait_ge(rf_root, 1)
            refine(P, slice(0, 3), rfr, rfm, rf, rf_step, 2)
            v.wait_ge(rf_step, 7)
            v.wait_ge(y_copied, 3 * (KT // 4 - 1))
            v.wait_ge(y_turned, KT)
            for h in range(4):
                c = slice(h * D // 4, (h + 1) * D // 4)
                src = yt[:, 0, c] if h < 3 else aux[0][:, :]
                v.tensor_scalar(yt[:, 0, c], src, rf[:, 0:1], None, ALU.mult).then_inc(y_done, 1)
            c = 3 * D // 4
            v.tensor_scalar(ys[:, 0:c], ys[:, 0:c], rf[0:NS, 2:3], None, ALU.mult)
            v.tensor_scalar(ys[:, c:D], aux[2][0:NS, :], rf[0:NS, 2:3], None, ALU.mult).then_inc(y_done, 1)

        @block.tensor
        def _(pe):
            def turn(out, in_, k):
                return pe.transpose(out, in_, ident[0:k, 0:k])

            pe.sem_inc(unit_used, RING)
            pe.wait_ge(const_done, 3)
            pe.wait_ge(params_in, 16 * 5)
            turn(aux[0][:, 0:6 * KT], var_rows[:, :], 6 * KT)
            for t in range(CW):
                c = 6 * KT + t * 2 * FT
                mm = turn(aux[0][:, c:c + 2 * FT], wf_rows[:, t, :], 2 * FT)
            mm.then_inc(params_turned, 1)

            def gates(k):
                if k == 0:
                    pe.wait_ge(gw_split, 6)
                pe.wait_ge(xl_done, k + 1)
                for t, (wt, xt) in enumerate(((gwh, xh), (gwh, xl), (gwl, xh))):
                    mm = pe.matmul(aux[1][0:GR, 0:NT], wt[:, k, :], xt[:, k, :], start=(k == 0 and t == 0),
                                   stop=(k == KT - 1 and t == 2))
                if k == KT - 1:
                    mm.then_inc(gz_done, 1)

            for k in range(KT):
                if k % (KT // 2) == 0:
                    pe.wait_ge(x_in[k // (KT // 2)], 16 * 5)
                if k >= RING:
                    pe.wait_ge(xh_done, k - RING + 1)
                for j in range(3):
                    r = P if j < 2 else TL
                    mm = turn(bank[k % RING][:, j * P:j * P + r], x_tok[0:r, j, k * P:(k + 1) * P], r)
                mm.then_inc(x_turned, 1)
                if k >= RING:
                    gates(k - RING)
            for k in range(KT - RING, KT):
                gates(k)

            def unit(u, slot, b, k0, kk, rh, rl, c0, c1, first, last, waits=()):
                pe.wait_ge(lo_done, u + 1 + RING)
                for k in range(kk):
                    for at_k, sm, value in waits:
                        if at_k == k:
                            pe.wait_ge(sm, value)
                    w = slice(k * P, (k + 1) * P)
                    for t, (wt, xt) in enumerate(((w_hi, rh), (w_hi, rl), (w_lo, rh))):
                        mm = pe.matmul(bank[b][:, 0:c1 - c0], wt[:, slot, w], xt[:, k0 + k, c0:c1],
                                       start=(first and k == 0 and t == 0), stop=(last and k == kk - 1 and t == 2))
                mm.then_inc(unit_used, 1)

            def strip(s, u, i, b, rh, rl, c0, c1, need=()):
                for h in range(2):
                    waits = [(k - h * KU, sm, x) for k, sm, x in need if k // KU == h]
                    if h == 1:
                        waits.append((2, evacuated, s + 2))
                    unit(u + h, (i + h) % RING, b, h * KU, KU, rh, rl, c0, c1, h == 0, h == 1, waits)

            def tiles_ready(done, per, start, n):
                return [(0, done, start + per * (n // 2)), (n // 2, done, start + per * (n - 2)),
                        (n - 2, done, start + per * (n - 1)), (n - 1, done, start + per * n)]

            def mix_strip(n, s, c0, c1, need=()):
                strip(n * 16 + s, n * HEAD_U + 2 * s, 2 * s, s % RING, xh, xl, c0, c1, need)

            def front(n, first=False):
                for s in range(4):
                    if first and s == 0:
                        mix_strip(n, 0, M0, NT, [(k, xl_done, k + 1) for k in range(KT)])
                        pe.wait_ge(fconv_in, 16)
                        for t in range(8):
                            mm = turn(aux[2 + t // 4][:, (t % 4) * P:(t % 4 + 1) * P], fc_rows[:, t, :], P)
                            if t % 4 == 3:
                                mm.then_inc(f_turned, 1)
                        for t in range(3):
                            mm = turn(aux[0][:, t * P:(t + 1) * P], fc_rows[:, 8 + t, :], P)
                        mm.then_inc(f_turned, 1)
                    else:
                        mix_strip(n, s, M0 if s == 0 else 0, NT)
                    if first and s == 1:
                        pe.wait_ge(copied, 4)
                        pe.wait_ge(diag_done, 3)
                        for j in range(3):
                            r = P if j < 2 else TL
                            mm = pe.matmul(aux[3][:, j * P:j * P + r], ones[0:r, :], diag[0:r, j, 0:r], start=True, stop=True)
                        mm.then_inc(r_spread, 1)
                        pe.wait_ge(states_in, 48)
                        for t in range(2):
                            turn(aux[2][:, t * P:(t + 1) * P], sc_rows[:, t, :], P)
                        turn(aux[2][:, 2 * P:2 * P + NS * H], n_rows[:, :], NS * H).then_inc(f_turned, 1)
                    if first and s == 3:
                        pe.wait_ge(r_done, 1)
                        pe.wait_ge(s_step, 3)
                        for j in range(3):
                            r = P if j < 2 else T2
                            mm = turn(aux[3][0:r, j * H:(j + 1) * H], a_row[:, j * P:j * P + r], H)
                        mm.then_inc(a_turned, 1)

            def back(n):
                for s in range(4, 16):
                    wide = (s - 4) % 6 < 2
                    mix_strip(n, s, C0 if wide else M0, NT)
                    if s == 4:
                        pe.wait_ge(evacuated, out_of(n * 16 + 3))
                        for c0, k0, nr, q0, nq in ((0, 0, P, 0, PM), (W1, P, P, Q1, PM - Q1), (W2, 2 * P, T2, Q2, T2)):
                            mm = pe.matmul(aux[0][0:nr, c0:c0 + nq], k_t[:, k0:k0 + nr], q_t[:, q0:q0 + nq],
                                           start=True, stop=True)
                        mm.then_inc(scores_done, 1)
                        for t in range(2):
                            for w in range(2):
                                turn(aux[1][:, t * DV + w * P:t * DV + (w + 1) * P], v_t[:, w, t * P:(t + 1) * P], P)
                            turn(aux[2][:, t * P:(t + 1) * P], k_t[:, t * P:(t + 1) * P], P)
                        for w in range(2):
                            turn(aux[2][0:T2, (2 + w) * P:(3 + w) * P], v_t[:, w, 2 * P:TP], P)
                            turn(aux[3][0:NS, (1 + w) * P:(2 + w) * P], v_t[:, w, TP:NT], P)
                        turn(aux[3][0:T2, 0:P], k_t[:, 2 * P:TP], P).then_inc(kv_turned, 1)
                    if s == 6:
                        pe.wait_ge(p_done, n + 1)
                        pe.wait_ge(c_in, n * 16 + 16)
                        for b in range(NS):
                            for w in range(2):
                                pe.matmul(aux[0][:, PM + w * NS + b:PM + w * NS + b + 1], c_st[:, b, w * P:(w + 1) * P],
                                          q_t[:, PM + b:PM + b + 1], start=True, stop=True)
                        pe.wait_ge(qk_done, n + 1)
                        pe.wait_ge(qn_done, n + 1)
                        pe.matmul(aux[0][:, PM + 2 * NS:PM + 4 * NS], ones[:, :], qp[:, :], start=True, stop=True)\
                          .then_inc(sample_done, 1)
                        pe.wait_ge(kv_done, n + 1)
                        for a in range(3):
                            for t, (c0, q0) in enumerate(((0, 0), (W1, Q1), (W2, Q2))):
                                lhs = ones[:, :] if a == 2 else v_tok[:, t, a * P:(a + 1) * P]
                                mm = pe.matmul(aux[a][:, q0:PM], lhs, pt[:, c0:c0 + PM - q0], start=(t == 0), stop=(t == 2))
                        mm.then_inc(num_done, 1)
                        for t in range(3):
                            mm = pe.matmul(aux[3][:, 0:DV + 1], kg[:, t, :], v_tok[:, t, :], start=(t == 0), stop=(t == 2))
                        mm.then_inc(cn_done, 1)

            front(0, first=True)
            pe.wait_ge(copied, 5)
            pe.wait_ge(const_done, 17)
            with pe.Fori(0, H - 1) as n:
                back(n)
                front(n + 1)
            back(H - 1)

            def out_strip(i, q, need=()):
                strip(i * 4 + (S_B + q), i * 8 + (U_B + 2 * q), 2 * q, q, mh, ml, 0, NM, need)

            out_strip(0, 0, tiles_ready(mix_split, 2, 0, KT))
            for q in range(1, 4):
                out_strip(0, q)
            with pe.Fori(1, KT // 4) as i:
                for q in range(4):
                    out_strip(i, q)
            pe.wait_ge(n_step, 2 * H)
            for t in range(NLAST):
                turn(aux[1 + t // 4][0:KT, (t % 4) * P:(t % 4 + 1) * P], cu_last[:, t, :], P)
            turn(aux[3][0:NS * H, 2 * P:3 * P], n_new[:, :, :].rearrange("p b h -> p (b h)"), P)
            turn(aux[3][0:H, 3 * P:4 * P], pn_new[:, :], P).then_inc(last_turned, 1)

            def up_strip(c, i, q, need=()):
                strip(i * 4 + (S_C + c * S_CH + q), i * 8 + (U_C + c * U_CH + 2 * q), 2 * q, q, xh, xl, 0, NM, need)

            def down_strip(c, i, q, need=(), bank_free=None):
                u = i * 12 + (U_C + c * U_CH + 4 * FC + 3 * q)
                for h, (k, kk) in enumerate(DOWN_UNITS):
                    waits = [(x - k, sm, value) for x, sm, value in need if k <= x < k + kk]
                    if h == 2 and bank_free is not None:
                        waits.append((2,) + bank_free)
                    unit(u + h, (3 * q + h) % RING, q, k, kk, hh, hl, 0, NF, h == 0, h == len(DOWN_UNITS) - 1, waits)

            for c in range(CH):
                if c == 0:
                    pe.wait_ge(acc_done, KT + 1)
                    pe.matmul(aux[0][:, 0:NM], ones[:, :], acc[:, :], start=True, stop=True).then_inc(r2_spread, 1)
                    up_strip(0, 0, 0, tiles_ready(x2g_step, 2, 1, KT))
                    for q in range(1, 4):
                        up_strip(0, 0, q)
                with pe.Fori(1 if c == 0 else 0, FC // 2) as i:
                    for q in range(4):
                        up_strip(c, i, q)
                s1 = S_C + c * S_CH + 2 * FC
                hid_need = tiles_ready(hid_split, 2, 2 * c * FC, FC)
                if c == 0:
                    for q in range(4):
                        down_strip(0, 0, q, hid_need if q == 0 else (), (evacuated, s1 + q + 2))
                    with pe.Fori(1, KT // 4) as i:
                        for q in range(4):
                            down_strip(0, i, q, (), (evacuated, i * 4 + (s1 + q + 2)))

            def turn_y(m):
                pe.wait_ge(x3_step, 2 * m + 2)
                if m % 4 == 0:
                    pe.wait_ge(up_copied, 3)
                    pe.wait_ge(y_copied, 3 * (m // 4))
                o = (m % 4) * P
                turn(aux[0][:, o:o + P], xg3[:, m % 2, 0:P], P)
                turn(aux[1][:, o:o + P], xg3[:, m % 2, P:2 * P], P)
                turn(aux[2][0:NS, o:o + P], xg3[:, m % 2, 2 * P:NF], P).then_inc(y_turned, 1)

            for m in range(KT):
                free = (evacuated, s1 + m + 2) if m < RING - 1 else (x3_step, 2 * (m + 1 - RING) + 1)
                down_strip(1, m // 4, m % 4, hid_need if m == 0 else (), free)
                if m == 0:
                    pe.wait_ge(last_copied, 2)
                    for t in range(NLAST):
                        mm = turn(aux[t // 4][0:2 * FT, (t % 4) * P:(t % 4 + 1) * P], up_last[:, t, :], P)
                        if t % 4 == 3 or t == NLAST - 1:
                            mm.then_inc(up_turned, 1)
                else:
                    turn_y(m - 1)
            turn_y(KT - 1)
            pe.wait_ge(acc_done, 2 * KT + 1)
            for j in range(3):
                r = P if j < 2 else NS
                mm = pe.matmul(aux[3][0:r, j:j + 1], acc[:, j * P:j * P + r], ones[:, 0:1], start=True, stop=True)
            mm.then_inc(ssqf_done, 1)


_INS = ['x_prompt', 'x_sample', 'state_mlstm_C', 'state_mlstm_n', 'state_mlstm_m', 'state_shortconv',
        'state_ffnconv', 'meta_tokens', 'norm1_g', 'w_in', 'b_if', 'w_shortconv', 'w_out', 'norm2_g',
        'w_up', 'w_ffconv', 'w_down', 'norm_f_g']


def out_shapes(a):
    depth, nb, heads, dk, dv = a['state_mlstm_C'].shape
    b, seq, d = a['x_prompt'].shape
    rows, ff2 = a['state_ffnconv'].shape[2:]
    return [(b, seq, d), a['x_sample'].shape, (depth, b, heads, dk, dv), (depth, b, heads, dk), (depth, b, heads),
            (depth, b, rows, d), (depth, b, rows, ff2), (depth, nb, heads, dk, dv), (depth, nb, heads, dk),
            (depth, nb, heads), (depth, nb, rows, d), (depth, nb, rows, ff2)]


def kernel(**inputs):
    import concourse.bacc as _bacc
    from concourse import mybir as _mybir
    from concourse.bass_utils import run_bass_kernel_spmd as _run
    f32 = _mybir.dt.float32
    arrays = {n: np.ascontiguousarray(inputs[n]) for n in _INS}
    nc = _bacc.Bacc("TRN2", target_bir_lowering=False, num_devices=1)
    ins = [nc.dram_tensor(f"in_{n}", arrays[n].shape, f32, kind="ExternalInput").ap() for n in _INS]
    outs = [nc.dram_tensor(f"out_{i}", s, f32, kind="ExternalOutput").ap() for i, s in enumerate(out_shapes(arrays))]
    nb, heads, _, dv = arrays['state_mlstm_C'].shape[1:]
    seq_w = arrays['x_prompt'].shape[1] + arrays['w_shortconv'].shape[1] - 1
    rows = nc.dram_tensor("scratch_rows", (heads, 2 * seq_w + 3 * nb), f32, kind="Internal").ap()
    vrows = nc.dram_tensor("scratch_v", (heads, nb * dv), f32, kind="Internal").ap()
    hybrid_decoder_step(nc, ins, outs, rows, vrows)
    r = _run(nc, [{f"in_{n}": arrays[n] for n in _INS}], core_ids=[0])
    return tuple(r.results[0][f"out_{i}"] for i in range(len(outs)))
```
